# Optimizing a Trainium2 kernel written in Bass

```python
import math, functools
import jax, jax.numpy as jnp
from jax import lax
import numpy as np

D_MODEL = 1024
BATCH = 1
SEQ = 512
DEPTH = 1
DEC_BATCH = 8
DEC_SEQ = 1
PAST_LEN = 2048
PAGE_SIZE = 128

DA_HEADS = D_MODEL // 256
DA_QK = 64
DA_V = 2 * DA_QK
DA_QCOLS = DA_HEADS * 2 * DA_QK
DA_COLS = 2 * DA_QCOLS + DA_HEADS * DA_V
DA_SCALE = DA_QK ** -0.5
RW_DIM = D_MODEL // 2
RW_HEAD = 64
RW_HEADS = RW_DIM // RW_HEAD
RW_W_LORA = 64
RW_A_LORA = 64
RW_G_LORA = 128
RW_PROJ = 3 * RW_DIM + RW_W_LORA + RW_A_LORA + RW_G_LORA
RW_GN_EPS = 64e-5
IN_COLS = DA_COLS + RW_PROJ
MIX_WIDTH = DA_HEADS * DA_V + RW_DIM
D_FF = ((8 * D_MODEL // 3 + 127) // 128) * 128
ROPE_THETA = 10000.0
QBLOCK = 128
ALPHA = (2 * DEPTH) ** 0.25
BETA = (8 * DEPTH) ** -0.25
LN_EPS = 1e-5
NEG = -1e30

kernel_name = 'hymba_diffattn_rwkv7_macaron_deepnorm_step'

def _layernorm(x, g, b):
    xf = x.astype(jnp.float32)
    mu = jnp.mean(xf, -1, keepdims=True)
    var = jnp.mean(jnp.square(xf - mu), -1, keepdims=True)
    return ((xf - mu) * lax.rsqrt(var + LN_EPS) * g + b).astype(x.dtype)

def _swiglu(x, w_gu, w_down):
    gate, up = jnp.split(x @ w_gu, 2, axis=-1)
    return (jax.nn.silu(gate) * up) @ w_down

def _rope(x, pos):
    half = DA_QK // 2
    inv = ROPE_THETA ** (-jnp.arange(half, dtype=jnp.float32) / half)
    ang = pos.astype(jnp.float32)[:, None] * inv[None, :]
    cos = jnp.cos(ang)[None, :, None, None, :]
    sin = jnp.sin(ang)[None, :, None, None, :]
    xf = x.astype(jnp.float32)
    x1, x2 = xf[..., :half], xf[..., half:]
    return jnp.concatenate([x1 * cos - x2 * sin, x2 * cos + x1 * sin], -1).astype(x.dtype)

def _diff_weights(logits, lam):
    p = jax.nn.softmax(logits, axis=-1)
    return p[:, :, 0] - lam * p[:, :, 1]

def _attn_prompt(q, k, v, lam):
    B, S = q.shape[0], q.shape[1]
    nb = S // QBLOCK
    qb = jnp.swapaxes(q.reshape(B, nb, QBLOCK, DA_HEADS, 2, DA_QK), 0, 1)
    kpos = jnp.arange(S)

    def one(args):
        q_blk, i = args
        qpos = i * QBLOCK + jnp.arange(QBLOCK)
        logits = jnp.einsum('bqhmd,bkhmd->bhmqk', q_blk, k,
                            preferred_element_type=jnp.float32) * DA_SCALE
        logits = jnp.where(kpos[None, :] <= qpos[:, None], logits, NEG)
        attn = _diff_weights(logits, lam).astype(v.dtype)
        return jnp.einsum('bhqk,bkhe->bqhe', attn, v)

    out = lax.map(one, (qb, jnp.arange(nb)))
    return jnp.swapaxes(out, 0, 1).reshape(B, S, DA_HEADS, DA_V)

def _attn_sample(q, k, v, lam, k_past, v_past):
    T = q.shape[1]
    P = k_past.shape[1]
    lp = jnp.einsum('bqhmd,bkhmd->bhmqk', q, k_past, preferred_element_type=jnp.float32)
    ln = jnp.einsum('bqhmd,bkhmd->bhmqk', q, k, preferred_element_type=jnp.float32)
    ln = jnp.where(jnp.tril(jnp.ones((T, T), dtype=bool)), ln, NEG)
    logits = jnp.concatenate([lp, ln], axis=-1) * DA_SCALE
    attn = _diff_weights(logits, lam).astype(v.dtype)
    return (jnp.einsum('bhqk,bkhe->bqhe', attn[..., :P], v_past)
            + jnp.einsum('bhqk,bkhe->bqhe', attn[..., P:], v))

def _rwkv7(prw, shift, wkv, p):
    B, T, _ = prw.shape
    dt = prw.dtype
    prev = jnp.concatenate([shift.astype(dt), prw[:, :-1]], axis=1)
    xm = (prw + (prev - prw) * p['rw_mu']).astype(jnp.float32)
    o1, o2, o3 = RW_DIM, 2 * RW_DIM, 3 * RW_DIM
    o4 = o3 + RW_W_LORA
    o5 = o4 + RW_A_LORA
    r, k, v = xm[..., :o1], xm[..., o1:o2], xm[..., o2:o3]
    xw, xa, xg = xm[..., o3:o4], xm[..., o4:o5], xm[..., o5:]
    w_log = -jax.nn.softplus(-(p['rw_w0'] + jnp.tanh(xw) @ p['rw_w2'])) - 0.5
    decay = jnp.exp(-jnp.exp(w_log))
    a = jax.nn.sigmoid(p['rw_a0'] + xa @ p['rw_a2'])
    g = jax.nn.sigmoid(xg) @ p['rw_g2']
    hs = (B, T, RW_HEADS, RW_HEAD)
    kk = (k * p['rw_k_k']).reshape(hs)
    kk = kk / jnp.maximum(jnp.sqrt(jnp.sum(kk * kk, -1, keepdims=True)), 1e-12)
    k = k * (1.0 + (a - 1.0) * p['rw_k_a'])
    r, k, v, decay, a = [t.reshape(hs) for t in (r, k, v, decay, a)]
    b = kk * a
    xs = tuple(jnp.swapaxes(t, 0, 1) for t in (r, decay, k, v, kk, b))

    def step(S, inp):
        r_t, w_t, k_t, v_t, kk_t, b_t = inp
        sa = jnp.einsum('bhvk,bhk->bhv', S, -kk_t)
        S = (S * w_t[:, :, None, :] + sa[..., None] * b_t[:, :, None, :]
             + v_t[..., None] * k_t[:, :, None, :])
        return S, jnp.einsum('bhvk,bhk->bhv', S, r_t)

    S_fin, o = lax.scan(step, wkv.astype(jnp.float32), xs)
    o = jnp.swapaxes(o, 0, 1)
    mu = jnp.mean(o, -1, keepdims=True)
    var = jnp.mean(jnp.square(o - mu), -1, keepdims=True)
    o = ((o - mu) * lax.rsqrt(var + RW_GN_EPS) * p['rw_lnx_g'].reshape(RW_HEADS, RW_HEAD)
         + p['rw_lnx_b'].reshape(RW_HEADS, RW_HEAD))
    o = o + jnp.sum(r * k * p['rw_r_k'], -1, keepdims=True) * v
    o = o.reshape(B, T, RW_DIM) * g
    return o.astype(dt), S_fin.astype(wkv.dtype), prw[:, -1:]

def _layer(x, p, lam_init, positions, attn_fn, shift, wkv):
    B, T, _ = x.shape
    h = _layernorm(ALPHA * x + 0.5 * _swiglu(x, p['ffa_w_gu'], p['ffa_w_down']),
                   p['ln1_g'], p['ln1_b'])
    proj = h @ p['w_in']
    q = _rope(proj[..., :DA_QCOLS].reshape(B, T, DA_HEADS, 2, DA_QK), positions)
    k = _rope(proj[..., DA_QCOLS:2 * DA_QCOLS].reshape(B, T, DA_HEADS, 2, DA_QK), positions)
    v = proj[..., 2 * DA_QCOLS:DA_COLS].reshape(B, T, DA_HEADS, DA_V)
    prw = proj[..., DA_COLS:]
    lq1, lk1 = p['da_lq1'].astype(jnp.float32), p['da_lk1'].astype(jnp.float32)
    lq2, lk2 = p['da_lq2'].astype(jnp.float32), p['da_lk2'].astype(jnp.float32)
    lam = jnp.exp(jnp.sum(lq1 * lk1)) - jnp.exp(jnp.sum(lq2 * lk2)) + lam_init
    o_da = attn_fn(q, k, v, lam).astype(jnp.float32)
    o_da = (o_da * lax.rsqrt(jnp.mean(o_da * o_da, -1, keepdims=True) + LN_EPS)
            * p['da_subln_g'] * (1.0 - lam_init))
    o_rw, wkv_new, shift_new = _rwkv7(prw, shift, wkv, p)
    mix = jnp.concatenate([o_da.reshape(B, T, DA_HEADS * DA_V).astype(x.dtype), o_rw],
                          axis=-1) @ p['w_out']
    h = _layernorm(ALPHA * h + mix, p['ln2_g'], p['ln2_b'])
    y = _layernorm(ALPHA * h + 0.5 * _swiglu(h, p['ffb_w_gu'], p['ffb_w_down']),
                   p['ln3_g'], p['ln3_b'])
    return y, k.reshape(B, T, DA_HEADS, 2 * DA_QK), v, wkv_new, shift_new

def setup_inputs(seed: int = 0) -> dict:
    key = jax.random.key(seed)
    ks = iter(jax.random.split(key, 64))

    def nrm(shape, scale):
        return jax.random.normal(next(ks), shape, jnp.float32) * scale

    n_pages = PAST_LEN // PAGE_SIZE
    n_used = DEC_BATCH * n_pages
    n_pool = n_used + max(1, n_used // 4)
    page_table = jax.random.permutation(next(ks), n_pool)[:n_used].reshape(
        DEC_BATCH, n_pages).astype(jnp.int32)
    col_scale = jnp.concatenate([
        jnp.ones((2 * DA_QCOLS,), jnp.float32),
        jnp.full((DA_HEADS * DA_V,), BETA, jnp.float32),
        jnp.ones((2 * RW_DIM,), jnp.float32),
        jnp.full((RW_DIM,), BETA, jnp.float32),
        jnp.ones((RW_W_LORA + RW_A_LORA + RW_G_LORA,), jnp.float32)])
    L = DEPTH
    return {
        'x_prompt': nrm((BATCH, SEQ, D_MODEL), 1.0),
        'x_sample': nrm((DEC_BATCH, DEC_SEQ, D_MODEL), 1.0),
        'cache_k': nrm((L, n_pool, PAGE_SIZE, DA_HEADS, 2 * DA_QK), 1.0),
        'cache_v': nrm((L, n_pool, PAGE_SIZE, DA_HEADS, DA_V), BETA),
        'state_wkv': nrm((L, DEC_BATCH, RW_HEADS, RW_HEAD, RW_HEAD), 0.5),
        'state_shift': nrm((L, DEC_BATCH, 1, RW_PROJ), 1.0),
        'page_table': page_table,
        'ffa_w_gu': nrm((L, D_MODEL, 2 * D_FF), D_MODEL ** -0.5),
        'ffa_w_down': nrm((L, D_FF, D_MODEL), BETA * D_FF ** -0.5),
        'ffb_w_gu': nrm((L, D_MODEL, 2 * D_FF), D_MODEL ** -0.5),
        'ffb_w_down': nrm((L, D_FF, D_MODEL), BETA * D_FF ** -0.5),
        'ln1_g': 1.0 + nrm((L, D_MODEL), 0.05),
        'ln1_b': nrm((L, D_MODEL), 0.01),
        'ln2_g': 1.0 + nrm((L, D_MODEL), 0.05),
        'ln2_b': nrm((L, D_MODEL), 0.01),
        'ln3_g': 1.0 + nrm((L, D_MODEL), 0.05),
        'ln3_b': nrm((L, D_MODEL), 0.01),
        'w_in': nrm((L, D_MODEL, IN_COLS), D_MODEL ** -0.5) * col_scale,
        'w_out': nrm((L, MIX_WIDTH, D_MODEL), BETA * MIX_WIDTH ** -0.5),
        'da_lq1': nrm((L, DA_QK), 0.1),
        'da_lk1': nrm((L, DA_QK), 0.1),
        'da_lq2': nrm((L, DA_QK), 0.1),
        'da_lk2': nrm((L, DA_QK), 0.1),
        'da_subln_g': 1.0 + nrm((L, DA_V), 0.05),
        'rw_mu': jax.random.uniform(next(ks), (L, RW_PROJ), jnp.float32),
        'rw_w0': jax.random.uniform(next(ks), (L, RW_DIM), jnp.float32, -5.0, 0.5),
        'rw_w2': nrm((L, RW_W_LORA, RW_DIM), 0.5 * RW_W_LORA ** -0.5),
        'rw_a0': nrm((L, RW_DIM), 0.1),
        'rw_a2': nrm((L, RW_A_LORA, RW_DIM), RW_A_LORA ** -0.5),
        'rw_g2': nrm((L, RW_G_LORA, RW_DIM), RW_G_LORA ** -0.5),
        'rw_k_k': 0.85 + nrm((L, RW_DIM), 0.05),
        'rw_k_a': 1.0 + nrm((L, RW_DIM), 0.05),
        'rw_r_k': nrm((L, RW_HEADS, RW_HEAD), 0.1),
        'rw_lnx_g': 1.0 + nrm((L, RW_DIM), 0.05),
        'rw_lnx_b': nrm((L, RW_DIM), 0.01),
    }

def reference(x_prompt, x_sample, cache_k, cache_v, state_wkv, state_shift, page_table,
              ffa_w_gu, ffa_w_down, ffb_w_gu, ffb_w_down,
              ln1_g, ln1_b, ln2_g, ln2_b, ln3_g, ln3_b,
              w_in, w_out, da_lq1, da_lk1, da_lq2, da_lk2, da_subln_g,
              rw_mu, rw_w0, rw_w2, rw_a0, rw_a2, rw_g2, rw_k_k, rw_k_a, rw_r_k,
              rw_lnx_g, rw_lnx_b):
    B, S, _ = x_prompt.shape
    DB, T, _ = x_sample.shape
    n_pages = page_table.shape[1]
    past = n_pages * PAGE_SIZE
    pos_prompt = jnp.arange(S)
    pos_sample = past + jnp.arange(T)
    y_prompt, y_sample = x_prompt, x_sample
    kp_l, vp_l, wp_l, sp_l, ks_l, vs_l, ws_l, ss_l = [], [], [], [], [], [], [], []
    for l in range(DEPTH):
        p = dict(ffa_w_gu=ffa_w_gu[l], ffa_w_down=ffa_w_down[l],
                 ffb_w_gu=ffb_w_gu[l], ffb_w_down=ffb_w_down[l],
                 ln1_g=ln1_g[l], ln1_b=ln1_b[l], ln2_g=ln2_g[l], ln2_b=ln2_b[l],
                 ln3_g=ln3_g[l], ln3_b=ln3_b[l], w_in=w_in[l], w_out=w_out[l],
                 da_lq1=da_lq1[l], da_lk1=da_lk1[l], da_lq2=da_lq2[l], da_lk2=da_lk2[l],
                 da_subln_g=da_subln_g[l], rw_mu=rw_mu[l], rw_w0=rw_w0[l],
                 rw_w2=rw_w2[l], rw_a0=rw_a0[l], rw_a2=rw_a2[l], rw_g2=rw_g2[l],
                 rw_k_k=rw_k_k[l], rw_k_a=rw_k_a[l], rw_r_k=rw_r_k[l],
                 rw_lnx_g=rw_lnx_g[l], rw_lnx_b=rw_lnx_b[l])
        lam_init = 0.8 - 0.6 * math.exp(-0.3 * l)
        shift0 = jnp.zeros((B, 1, RW_PROJ), x_prompt.dtype)
        wkv0 = jnp.zeros((B, RW_HEADS, RW_HEAD, RW_HEAD), x_prompt.dtype)
        y_prompt, kp, vp, wp, sp = _layer(y_prompt, p, lam_init, pos_prompt,
                                          _attn_prompt, shift0, wkv0)
        k_past = cache_k[l][page_table].reshape(DB, past, DA_HEADS, 2, DA_QK)
        v_past = cache_v[l][page_table].reshape(DB, past, DA_HEADS, DA_V)
        attn_fn = functools.partial(_attn_sample, k_past=k_past, v_past=v_past)
        y_sample, ks, vs, ws, ss = _layer(y_sample, p, lam_init, pos_sample, attn_fn,
                                          state_shift[l], state_wkv[l])
        kp_l.append(kp); vp_l.append(vp); wp_l.append(wp); sp_l.append(sp)
        ks_l.append(ks); vs_l.append(vs); ws_l.append(ws); ss_l.append(ss)
    k_prompt = jnp.stack(kp_l)
    v_prompt = jnp.stack(vp_l)
    wkv_prompt = jnp.stack(wp_l)
    shift_prompt = jnp.stack(sp_l)
    k_sample = jnp.stack(ks_l)
    v_sample = jnp.stack(vs_l)
    wkv_sample = jnp.stack(ws_l)
    shift_sample = jnp.stack(ss_l)
    return (y_prompt, y_sample, k_prompt, v_prompt, wkv_prompt, shift_prompt,
            k_sample, v_sample, wkv_sample, shift_sample)


_drawn_inputs = setup_inputs


def setup_inputs(seed=0):
    import zlib

    import numpy as np

    out = dict(_drawn_inputs(seed))
    spreads = {}
    factors = {'ln2_b': 5.68,
     'ln3_b': 5.719,
     'da_lq1': 8.0,
     'da_lk1': 8.0,
     'da_lq2': 6.845,
     'da_lk2': 8.0,
     'da_subln_g': 3.812,
     'rw_lnx_g': 6.495,
     'rw_lnx_b': 56.115}
    for name, (base, spread) in spreads.items():
        noise = np.random.default_rng([zlib.crc32(name.encode()), seed]).standard_normal(out[name].shape)
        drawn = base * np.exp(spread * noise) if base else spread * noise
        out[name] = __import__('jax').numpy.asarray(drawn.astype(out[name].dtype))
    for name, factor in factors.items():
        out[name] = (out[name] * factor).astype(out[name].dtype)
    return out
```

```python
import math
import numpy as np
import concourse.bass as bass
from concourse import mybir
from contextlib import ExitStack

P = 128
D_MODEL, SEQ, DEC = 1024, 512, 8
TOK = SEQ + DEC
HALF = TOK // 2
DC = D_MODEL // P
D_FF = 2816
FC = D_FF // P
DA_HEADS, DA_QK = 4, 64
RW_DIM, RW_PROJ = 512, 1792
RC = RW_PROJ // P
IN_CHUNKS = 3 * DA_HEADS + RC
PAST, PAGE = 2048, 128
PAGES = PAST // PAGE
POOL = 160
ALPHA = 2 ** 0.25
LN_EPS = 1e-5
GN_EPS = 64e-5
LAM_INIT = 0.8 - 0.6 * math.exp(-0.0)
SCALE = DA_QK ** -0.5
NEG = -1e30
CH = 64
NCH = SEQ // CH
LEVELS = (1, 2, 4, 8, 16, 32)
DOWN_K = (6, 6, 5, 5)

C_ID, C_SWAP, C_CAUSAL, C_STRICT, C_INCL, C_HEAD = (P * n for n in range(6))
C_LOW1 = P * 6
C_LEV = P * 7
C_KEEP = C_LEV + P * len(LEVELS)
NCONST = C_KEEP + SEQ

V_LN = 0
V_SUB = V_LN + 6 * DC
V_MU2 = V_SUB + 1
V_PAIR = V_MU2 + 2
NVEC = V_PAIR + 40
KS, VS = 4, 4


class Product:

    def __init__(self, body, times, before=None):
        self.body, self.times = body, times
        self.block0 = before.block0 + before.times * len(before.body) if before else 0
        used = [0] * 4
        for _, _, sets, begins, _ in body:
            for s in sets:
                used[s] += begins
        self.used = used
        self.used0 = [a + before.times * b for a, b in zip(before.used0, before.used)] if before else [0] * 4
        self.slabs = 2 * len(body)

    def block(self, i, b):
        return i * len(self.body) + (self.block0 + b)

    def raw_slot(self, b):
        return (self.block0 + b) % 2

    def raw_count(self, i, b):
        return i * (8 * len(self.body)) + 16 * ((self.block0 + b) // 2 + 1)

    def slab(self, i, k):
        return i * self.slabs + (2 * self.block0 + k)

    def slot(self, k):
        return (2 * self.block0 + k) % 4

    def set_uses(self, i, k):
        s = self.body[k // 2][2][k % 2]
        begun = sum(blk[3] for blk in self.body[:k // 2 + 1] if s in blk[2])
        return i * self.used[s] + (self.used0[s] + begun - 1)


PAIR_BODY = [(0, DC, (0, 1), True, True), (0, DC, (2, 3), True, True)]
DOWN_BODY = [(sum(DOWN_K[:r]), DOWN_K[r], sets, r == 0, r == 3) for sets in ((0, 1), (2, 3)) for r in range(4)]


def wait_from_one(eng, sem, value):
    if not isinstance(value, int) or value > 0:
        eng.wait_ge(sem, value)


def layer(nc, x_in, gu_a, down_a, w_in, w_out, gu_b, down_b, consts, vecs, lams, lora, g2,
          cache_k, cache_v, pages, state_in, shift_in,
          y_out, k_out, v_out, wkv_out, shift_out, wkv_s_out):
    f32, f32r, i32 = mybir.dt.float32, mybir.dt.float32r, mybir.dt.int32
    ALU, ACT, AX = mybir.AluOpType, mybir.ActivationFunctionType, mybir.AxisListType

    up_a = Product(PAIR_BODY, FC // 2)
    dn_a = Product(DOWN_BODY, 2, up_a)
    inp = Product(PAIR_BODY, 6, dn_a)
    inp_tail = Product(PAIR_BODY[:1], 1, inp)
    outp = Product(PAIR_BODY, 2, inp_tail)
    up_b = Product(PAIR_BODY, FC // 2, outp)
    dn_b = Product(DOWN_BODY, 2, up_b)

    hi_dram = nc.dram_tensor("trunk_hi", (P, DC, TOK), f32, kind="Internal").ap()
    lo_dram = nc.dram_tensor("trunk_lo", (P, DC, TOK), f32, kind="Internal").ap()

    ctx = ExitStack()
    with ctx:
        def sb(name, shape, dt=f32, to=ctx):
            return to.enter_context(nc.sbuf_tensor(name, shape, dt))

        def sem(name):
            return ctx.enter_context(nc.semaphore(name))

        acc = [ctx.enter_context(nc.psum_tensor(f"acc{n}", [P, 2, 512], f32)) for n in range(4)]

        trunk = ExitStack()
        XH = sb("x_hi", [P, DC, TOK], f32r, trunk)
        XL = sb("x_lo", [P, DC, TOK], f32r, trunk)
        RAW = [sb(f"weights_raw{n}", [P, DC, 2 * P], f32, trunk) for n in range(2)]
        WH = [sb(f"weights_hi{n}", [P, DC, P], f32r, trunk) for n in range(4)]
        WL = [sb(f"weights_lo{n}", [P, DC, P], f32r, trunk) for n in range(4)]
        trunk.close()
        mixing = ExitStack()
        U = sb("head_tiles", [P, 11, TOK], f32, mixing)
        BD = [sb(f"blocks_{n}", [P, NCH, P], f32, mixing) for n in "abkrv"]
        TT, MT, RBT, RKT, PP, PT, YY, EE = (
            sb(n, [P, NCH, P], f32, mixing)
            for n in ("t_turned", "m_turned", "rb_turned", "rk_turned", "inverse", "inverse_turned", "level_y", "level_e"))
        TK = {n: sb(f"tokens_{c}", [P, NCH, P], f32, mixing) for n, c in ((1, "b"), (2, "k"), (4, "v"))}
        ST = sb("state", [P, 2, P], f32, mixing)
        SG, UN, SA = (sb(n, [P, P], f32, mixing) for n in ("state_gained", "minus_u", "sa"))
        mixing.close()
        region = sb("first_region", [P, 4 * (11 * TOK + (5 + 8 + 3) * NCH * P + 5 * P)], mybir.dt.uint8)

        Y = sb("y_sum", [P, DC, TOK])
        SCR = sb("scratch", [P, 6, TOK])
        VEC = sb("feature_vectors", [P, NVEC])
        MEAN = sb("mean_weights", [P, P])
        EPS = sb("epsilons", [P, 5])
        COS, SIN = Y[:, 6, :], Y[:, 7, :]

        ffn = ExitStack()
        HH = sb("hidden_hi", [P, FC, TOK], f32r, ffn)
        HL = sb("hidden_lo", [P, FC, TOK], f32r, ffn)
        ffn.close()
        mixed = ExitStack()
        MH = sb("mixed_hi", [P, DC, TOK], f32r, mixed)
        ML = sb("mixed_lo", [P, DC, TOK], f32r, mixed)
        mixed.close()
        PROJ = sb("projected", [P, IN_CHUNKS, TOK])
        CONST = sb("constants", [P, NCONST])
        KP = sb("key_pages", [P, KS, 512])
        VP = sb("value_pages", [P, VS, 512])
        QB = sb("query_rows", [P, 512])
        XWA = sb("decay_rate_inputs", [P, TOK])
        XSG = sb("gate_inputs", [P, TOK])
        LORA, LG2 = sb("lora_w2_a2", [P, P]), sb("lora_g2", [P, P])
        LAMV, LAM = sb("lambda_vectors", [P, 256]), sb("lambda", [P, 8])
        SHIFT = sb("shift_rows", [P, RC, DEC])
        QK, OWN = sb("own_key_products", [P, 4, DEC]), sb("own_logits", [P, DEC, 4, 2])
        ID2 = sb("stacked_identity", [P, 64])
        TABLE = sb("page_ids", [1, DEC * PAGES], i32)
        L, SM = sb("decode_logits", [P, PAGES + 1, 8]), sb("decode_small", [P, 32])
        AD = sb("decode_weights", [P, PAGES + 1, 4])
        SMP = sb("prompt_small", [P, 8])
        PV, PVS, GAIN = sb("pair_vectors", [P, 10]), sb("pair_vectors_s", [P, 10]), sb("gains", [P, NCH])

        sems = {}

        def g(name):
            if name not in sems:
                sems[name] = sem(name)
            return sems[name]

        raw_ready = [sem(f"raw_ready{n}") for n in range(2)]
        split_hi, split_lo, slab_used = sem("split_hi"), sem("split_lo"), sem("slab_used")
        acc_free = [sem(f"acc_free{n}") for n in range(4)]
        tables_in, x_loaded, consts_set = sem("tables_in"), sem("x_loaded"), sem("consts_set")
        x_hi, x_ready = sem("x_hi_done"), sem("x_ready")
        gated, hidden, h_hi, h_ready = sem("gated"), sem("hidden"), sem("h_hi"), sem("h_ready")
        y_ready, y_part = sem("y_ready"), sem("y_part")
        mean_done, centered, squared, var_done, std_done, rstd_done, scaled = (
            sem(n) for n in ("mean_done", "centered", "squared", "var_done", "std_done", "rstd_done", "scaled"))
        stored = sem("stored")
        proj_ready = sem("proj_ready")

        def halves(t):
            return t.rearrange("p (a n) -> p a n", a=2)

        def accv(s):
            return acc[s][:, :, 0:HALF]

        def load_weights(sp, pr, i, src):
            for b, (k0, nk, _, _, _) in enumerate(pr.body):
                wait_from_one(sp, split_lo, 2 * (pr.block(i, b) - 1))
                slot = pr.raw_slot(b)
                sp.dma_start(RAW[slot][:, 0:nk, :], src(i, b)).then_inc(raw_ready[slot], 16)

        def split_high(act, pr, i, k):
            b = k // 2
            nk, slot = pr.body[b][1], pr.raw_slot(b)
            act.wait_ge(raw_ready[slot], pr.raw_count(i, b))
            wait_from_one(act, slab_used, pr.slab(i, k) - 3)
            nc.scalar.activation(WH[pr.slot(k)][:, 0:nk, :], RAW[slot][:, 0:nk, P * (k % 2):P * (k % 2) + P],
                                 ACT.Copy).then_inc(split_hi, 1)

        def split_low(dve, pr, i, k):
            b = k // 2
            nk, slot = pr.body[b][1], pr.raw_slot(b)
            dve.wait_ge(split_hi, pr.slab(i, k) + 1)
            nc.vector.tensor_tensor(WL[pr.slot(k)][:, 0:nk, :], RAW[slot][:, 0:nk, P * (k % 2):P * (k % 2) + P],
                                    WH[pr.slot(k)][:, 0:nk, :].bitcast(f32), ALU.subtract).then_inc(split_lo, 1)

        def multiply(pe, pr, i, hi, lo):
            for k in range(pr.slabs):
                k0, nk, sets, begins, ends = pr.body[k // 2]
                s, slot = sets[k % 2], pr.slot(k)
                pe.wait_ge(split_lo, pr.slab(i, k) + 1)
                if begins:
                    wait_from_one(pe, acc_free[s], pr.set_uses(i, k))
                for t in range(nk):
                    for n, (w, x) in enumerate(((WH, hi), (WH, lo), (WL, hi))):
                        for a in range(2):
                            mm = nc.tensor.matmul(acc[s][:, a, 0:HALF], w[slot][:, t, :],
                                                  x[:, k0 + t, HALF * a:HALF * a + HALF],
                                                  start=begins and t == 0 and n == 0,
                                                  stop=ends and t == nk - 1 and n == 2)
                mm.then_inc(slab_used, 1)

        def gate_up_scalar(act, pr, u, i, split, drain):
            for k in range(4):
                if split:
                    split_high(act, pr, i, k)
                if drain and k < 2:
                    act.wait_ge(slab_used, pr.slab(i - 1, k) + 1)
                    wait_from_one(act, hidden, 2 * (i - 2) + k + 1 + u * FC)
                    nc.scalar.activation(halves(SCR[:, k, :]), accv(k), ACT.Silu).then_inc(acc_free[k], 1)
                if drain and k >= 2:
                    act.wait_ge(hidden, 2 * (i - 1) + k - 1 + u * FC)
                    nc.scalar.activation(HH[:, bass.ds(2 * (i - 1) + k - 2, 1), :], SCR[:, k:k + 1, :],
                                         ACT.Copy).then_inc(h_hi, 1)

        def gate_up_vector(dve, pr, u, i, split, drain):
            for k in range(4):
                if split:
                    split_low(dve, pr, i, k)
                if drain and k >= 2:
                    c = 2 * (i - 1) + k - 2
                    dve.wait_ge(acc_free[k - 2], pr.set_uses(i - 1, k - 2) + 1)
                    dve.wait_ge(slab_used, pr.slab(i - 1, k) + 1)
                    dve.tensor_tensor(halves(SCR[:, k, :]), halves(SCR[:, k - 2, :]), accv(k),
                                      ALU.mult).then_inc(hidden, 1)
                    dve.wait_ge(h_hi, c + 1 + u * FC)
                    dve.tensor_tensor(HL[:, bass.ds(c, 1), :], SCR[:, k:k + 1, :],
                                      HH[:, bass.ds(c, 1), :].bitcast(f32), ALU.subtract).then_inc(acc_free[k], 1)

        def residual(dve, pr, i, k, c, coef):
            s = pr.body[k // 2][2][k % 2]
            dve.wait_ge(slab_used, pr.slab(i, k) + 1)
            chunk = halves(Y[:, bass.ds(c, 1), :].rearrange("p a n -> p (a n)"))
            xh = halves(XH[:, bass.ds(c, 1), :].rearrange("p a n -> p (a n)").bitcast(f32))
            xl = halves(XL[:, bass.ds(c, 1), :].rearrange("p a n -> p (a n)").bitcast(f32))
            nc.vector.scalar_tensor_tensor(out=chunk, in0=xh, scalar=coef, in1=accv(s), op0=ALU.mult,
                                           op1=ALU.add).then_inc(acc_free[s], 1)
            dve.wait_ge(acc_free[s], pr.set_uses(i, k) + 1)
            nc.vector.scalar_tensor_tensor(out=chunk, in0=xl, scalar=coef, in1=chunk, op0=ALU.mult,
                                           op1=ALU.add).then_inc(y_ready, 1)

        def down_tensor(pe, pr, u):
            for s in (2, 3):
                pe.wait_ge(acc_free[s], pr.used0[s])
            with pe.Fori(0, pr.times) as i:
                multiply(pe, pr, i, HH, HL)

        def down_scalar(act, pr):
            with act.Fori(0, pr.times) as i:
                for k in range(pr.slabs):
                    split_high(act, pr, i, k)

        def down_vector(dve, pr):
            with dve.Fori(0, pr.times) as i:
                for k in range(pr.slabs):
                    split_low(dve, pr, i, k)
                    for e, c in ((6, 0), (7, 1), (14, 2), (15, 3)):
                        if k == min(e + 4, pr.slabs - 1):
                            residual(dve, pr, i, e, i * 4 + c, 2 * ALPHA)

        def norm_tensor(pe, n):
            pe.wait_ge(y_ready, DC * n + 6)
            for c in range(DC):
                pe.wait_ge(y_ready, DC * n + c + 1)
                for a in range(2):
                    mm = nc.tensor.matmul(acc[0][:, a, 0:HALF], MEAN[:, :], Y[:, c, HALF * a:HALF * a + HALF],
                                          start=c == 0, stop=c == DC - 1)
            mm.then_inc(mean_done, 1)
            for c in range(DC):
                pe.wait_ge(squared, DC * n + c + 1)
                for a in range(2):
                    mm = nc.tensor.matmul(acc[1][:, a, 0:HALF], MEAN[:, :],
                                          SCR[:, 2 + c % 2, HALF * a:HALF * a + HALF],
                                          start=c == 0, stop=c == DC - 1)
                mm.then_inc(var_done, 1)

        def norm_scalar(act, n, out=None):
            for c in range(DC):
                act.wait_ge(centered, DC * n + c + 1)
                if DC * n + c >= 2:
                    act.wait_ge(var_done, DC * n + c - 1)
                nc.scalar.activation(SCR[:, 2 + c % 2, :], Y[:, c, :], ACT.Square).then_inc(squared, 1)
            act.wait_ge(var_done, DC * n + DC)
            nc.scalar.activation(halves(SCR[:, 4, :]), accv(1), ACT.Sqrt, bias=EPS[:, n:n + 1]).then_inc(std_done, 1)
            for c in range(DC):
                act.wait_ge(scaled, DC * n + c + 1)
                bias = VEC[:, V_LN + (2 * n + 1) * DC + c:V_LN + (2 * n + 1) * DC + c + 1]
                if out is None:
                    nc.scalar.activation(XH[:, c, :], Y[:, c, :], ACT.Identity, bias=bias).then_inc(x_hi, 1)
                else:
                    nc.scalar.activation(Y[:, c, :], Y[:, c, :], ACT.Identity, bias=bias).then_inc(x_hi, 1)

        def norm_vector(dve, n, last=False):
            dve.wait_ge(mean_done, n + 1)
            for c in range(DC):
                nc.vector.tensor_tensor(halves(Y[:, c, :]), halves(Y[:, c, :]), accv(0),
                                        ALU.subtract).then_inc(centered, 1)
            dve.wait_ge(std_done, n + 1)
            nc.vector.reciprocal(SCR[:, 5, :], SCR[:, 4, :]).then_inc(rstd_done, 1)
            dve.wait_ge(rstd_done, n + 1)
            for c in range(DC):
                g = V_LN + 2 * n * DC + c
                nc.vector.scalar_tensor_tensor(out=Y[:, c, :], in0=Y[:, c, :], scalar=VEC[:, g:g + 1],
                                               in1=SCR[:, 5, :], op0=ALU.mult, op1=ALU.mult).then_inc(scaled, 1)
                if not last and c >= 1:
                    low_part(dve, n, c - 1)
            if not last:
                low_part(dve, n, DC - 1)

        def low_part(dve, n, c):
            b = V_LN + (2 * n + 1) * DC + c
            dve.wait_ge(x_hi, DC * (n + 1) + c + 1)
            nc.vector.scalar_tensor_tensor(out=XL[:, c, :], in0=Y[:, c, :], scalar=VEC[:, b:b + 1],
                                           in1=XH[:, c, :].bitcast(f32), op0=ALU.add,
                                           op1=ALU.subtract).then_inc(x_ready, 1)

        def to_projected(act, pr, i, k, c):
            act.wait_ge(slab_used, pr.slab(i, k) + 1)
            nc.scalar.activation(halves(PROJ[:, bass.ds(c, 1), :].rearrange("p a n -> p (a n)")),
                                 accv(pr.body[k // 2][2][k % 2]), ACT.Copy)\
                .then_inc(acc_free[pr.body[k // 2][2][k % 2]], 1)

        def input_scalar(act):
            def step(i, split, drain):
                for k in range(4):
                    if split:
                        split_high(act, inp, i, k)
                    if drain:
                        to_projected(act, inp, i - 1, k, (i - 1) * 4 + k)
            step(0, True, False)
            with act.Fori(1, inp.times) as i:
                step(i, True, True)
            for k in range(4):
                if k < 2:
                    split_high(act, inp_tail, 0, k)
                to_projected(act, inp, inp.times - 1, k, 4 * (inp.times - 1) + k)
            for k in range(2):
                to_projected(act, inp_tail, 0, k, 4 * inp.times + k)

        def gate_up(step, eng, pr, u):
            step(eng, pr, u, 0, True, False)
            step(eng, pr, u, 1, True, True)
            with eng.Fori(2, pr.times) as i:
                step(eng, pr, u, i, True, True)
            step(eng, pr, u, pr.times, False, True)

        def gate_up_tensor(pe, pr, n):
            pe.wait_ge(x_ready, DC * (n + 1))
            multiply(pe, pr, 0, XH, XL)
            with pe.Fori(1, pr.times) as i:
                multiply(pe, pr, i, XH, XL)

        def pj(c):
            return PROJ[:, bass.ds(c, 1), :].rearrange("p a n -> p (a n)")

        def projected(eng):
            for s in range(4):
                eng.wait_ge(acc_free[s], outp.used0[s])

        def const(c, n=P):
            return CONST[:, c:c + n]

        def bank(n):
            return acc[n // 2][:, n % 2, :]

        def shift(dve, chain, out, c, last, mu):
            tmp, cur = SCR[:, 5, :], pj(c)
            nc.vector.tensor_tensor(tmp[:, 1:SEQ], cur[:, 0:SEQ - 1], cur[:, 1:SEQ], ALU.subtract)
            nc.vector.tensor_scalar(tmp[:, 0:1], cur[:, 0:1], -1.0, None, ALU.mult)
            chain(nc.vector.tensor_tensor(tmp[:, SEQ:TOK], last, cur[:, SEQ:TOK], ALU.subtract))
            return nc.vector.scalar_tensor_tensor(out=out, in0=tmp, scalar=mu, in1=cur, op0=ALU.mult, op1=ALU.add)

        class Chain:

            def __init__(self, eng, sem, turn=0, per_turn=0, before=0):
                self.eng, self.sem, self.turn, self.per_turn, self.n, self.before = eng, sem, turn, per_turn, 0, before

            def __call__(self, ins):
                self.n += 1
                ins.then_inc(self.sem, 1)
                self.eng.wait_ge(self.sem, self.turn * self.per_turn + (self.before + self.n))

            def end(self):
                assert self.n == self.per_turn, (self.sem.name, self.n)

        def prelude_tensor(pe):
            projected(pe)
            pe.wait_ge(g("consts_in"), 16)
            for c in range(2 * DA_HEADS):
                if c >= 4:
                    pe.wait_ge(g("rope_sin"), c - 3)
                for a in range(2):
                    mm = nc.tensor.matmul(acc[c % 4][:, a, 0:HALF], const(C_SWAP), PROJ[:, c, HALF * a:HALF * a + HALF],
                                          start=True, stop=True)
                mm.then_inc(g("rope_swapped"), 1)
            pe.wait_ge(g("own_products"), 1)
            for m in range(2):
                mm = nc.tensor.matmul(bank(m)[:, 0:32], MEAN[64 * m:64 * m + 64, :], QK[64 * m:64 * m + 64, :, :],
                                      start=True, stop=True)
            mm.then_inc(g("own_summed"), 1)

        def prelude_pool(pool):
            projected(pool)
            pool.wait_ge(g("consts_in"), 16)
            for c in range(2 * DA_HEADS):
                if c >= 2:
                    pool.wait_ge(g("roped"), c - 1)
                pool.tensor_tensor(SCR[:, 2 + c % 2, :], PROJ[:, c, :], COS, ALU.mult).then_inc(g("rope_cos"), 1)
                pool.wait_ge(g("rope_cos"), c + 1)
                pool.wait_ge(g("rope_sin"), c + 1)
                pool.tensor_tensor(PROJ[:, c, :], SCR[:, c % 2, :], SCR[:, 2 + c % 2, :], ALU.add).then_inc(g("roped"), 1)

        def prelude_vector(dve):
            projected(dve)
            dve.wait_ge(g("consts_in"), 16)
            dve.wait_ge(g("small_in"), 48)
            chain = Chain(dve, g("dve_prelude"))
            nc.vector.tensor_tensor(LAMV[:, 0:64], LAMV[:, 0:64], LAMV[:, 64:128], ALU.mult)
            chain(nc.vector.tensor_tensor(LAMV[:, 128:192], LAMV[:, 128:192], LAMV[:, 192:256], ALU.mult))
            nc.vector.reduce_sum(LAM[:, 0:1], LAMV[:, 0:64], AX.X)
            nc.vector.reduce_sum(LAM[:, 1:2], LAMV[:, 128:192], AX.X).then_inc(g("lam_sums"), 1)
            nc.vector.tensor_tensor(ID2[:, :], const(C_ID, 64), const(C_ID + 64, 64), ALU.add)
            for c in range(2 * DA_HEADS):
                dve.wait_ge(g("rope_swapped"), c + 1)
                if c >= 2:
                    dve.wait_ge(g("roped"), c - 1)
                nc.vector.tensor_tensor(halves(SCR[:, c % 2, :]), accv(c % 4), halves(SIN),
                                        ALU.mult).then_inc(g("rope_sin"), 1)
            dve.wait_ge(g("lam_exps"), 1)
            chain(nc.vector.tensor_tensor(LAM[:, 0:1], LAM[:, 3:4], LAM[:, 2:3], ALU.subtract))
            chain(nc.vector.tensor_scalar(LAM[:, 4:5], LAM[:, 0:1], -LAM_INIT, None, ALU.add))
            chain(shift(dve, chain, XWA[:, :], 24, SHIFT[:, 12, :], VEC[:, V_MU2:V_MU2 + 1]))
            shift(dve, chain, XSG[:, :], 25, SHIFT[:, 13, :], VEC[:, V_MU2 + 1:V_MU2 + 2]).then_inc(g("lora_in"), 1)
            dve.wait_ge(g("roped"), 8)
            nc.vector.tensor_tensor(QK[:, :, :], PROJ[:, 0:4, SEQ:TOK], PROJ[:, 4:8, SEQ:TOK],
                                    ALU.mult).then_inc(g("own_products"), 1)
            nc.vector.memset(SG[:, :], 0.0).then_inc(g("d_out"), 1)
            dve.wait_ge(g("own_summed"), 1)
            for m in range(2):
                ins = nc.vector.tensor_scalar(OWN[:, :, :, m].rearrange("p b h -> p h b"),
                                              bank(m)[:, 0:32].rearrange("p (h b) -> p h b", b=DEC),
                                              float(D_MODEL), None, ALU.mult)
            ins.then_inc(g("own_ready"), 1)

        def prelude_scalar(act):
            act.wait_ge(g("lam_sums"), 1)
            nc.scalar.activation(LAM[:, 2:4], LAM[:, 0:2], ACT.Exp).then_inc(g("lam_exps"), 1)
            act.wait_ge(g("lora_in"), 1)
            nc.scalar.activation(XWA[0:64, :], XWA[0:64, :], ACT.Tanh)
            nc.scalar.activation(XSG[:, :], XSG[:, :], ACT.Sigmoid).then_inc(g("lora_act"), 1)

        def decode_loads(sp):
            def page(b, n, cache, dst, done):
                pid = sp.value_load(TABLE[0:1, bass.ds(b * PAGES + n, 1)], min_val=0, max_val=POOL - 1)
                sp.dma_start(dst, cache[bass.ds(pid, 1), :, :].rearrange("a p n -> (a p) n")).then_inc(done, 16)

            def k_page(b, n):
                wait_from_one(sp, g("k_reduced"), b * PAGES + (n - KS + 1))
                page(b, n, cache_k, KP[:, n % KS, :], g(f"k_in{n % KS}"))

            def v_page(b, n):
                wait_from_one(sp, g("v_used"), b * PAGES + (n - VS + 1))
                page(b, n, cache_v, VP[:, n % VS, :], g(f"v_in{n % VS}"))

            for n in range(PAGES):
                k_page(0, n)

            def turn(b):
                for n in range(PAGES):
                    v_page(b, n)
                    if n < KS:
                        k_page(b + 1, n)
                for n in range(KS, PAGES):
                    k_page(b + 1, n)
            turn(0)
            with sp.Fori(1, DEC - 1) as b:
                turn(b)
            for n in range(PAGES):
                v_page(DEC - 1, n)

        def decode_query_pool(pool, b):
            pool.tensor_copy(QB[:, :].rearrange("p (h n) -> p h n", n=P), PROJ[:, 0:4, bass.ds(b + SEQ, 1)].broadcast_to([P, 4, P]))\
                .then_inc(g("q_column"), 1)

        def decode_query_tensor(pe, b, bk):
            pe.wait_ge(g("q_column"), b + 1)
            pe.wait_ge(g("d_out"), b + 1)
            for h in range(DA_HEADS):
                mm = nc.tensor.matmul(bank(bk)[:, P * h:P * h + P], QB[:, P * h:P * h + P], const(C_ID), start=True, stop=True)
            mm.then_inc(g("q_spread"), 1)

        def decode_query_scalar(act, b, bk):
            act.wait_ge(g("q_spread"), b + 1)
            nc.scalar.activation(QB[:, :], bank(bk), ACT.Copy).then_inc(g("q_rows"), 1)

        def decode_pages_pool(pool, b, pages):
            pool.wait_ge(g("q_rows"), b + 1)
            for n in pages:
                pool.wait_ge(g(f"k_in{n % KS}"), b * (16 * PAGES // KS) + 16 * (n // KS + 1))
                pool.tensor_tensor(KP[:, n % KS, :], KP[:, n % KS, :], QB[:, :], ALU.mult).then_inc(g("k_multiplied"), 1)
                if n == PAGES - 1:
                    pool.wait_ge(g("k_multiplied"), b * PAGES + PAGES)

        def decode_pages_vector(dve, b, pages):
            for n in pages:
                dve.wait_ge(g("k_multiplied"), b * PAGES + (n + 1))
                nc.vector.reduce_sum(L[:, n, :], KP[:, n % KS, :].rearrange("p (g d) -> p g d", d=DA_QK),
                                     AX.X).then_inc(g("k_reduced"), 1)

        def decode_softmax_vector(dve, b, bk, chain):
            chain(nc.vector.tensor_copy(L[:, PAGES, :], OWN[:, bass.ds(b, 1), :, :].rearrange("p b h m -> p (b h m)")))
            nc.vector.reduce_max(SM[:, 0:8], L[:, :, :].rearrange("p n g -> p g n"), AX.X).then_inc(g("max_part"), 1)
            dve.wait_ge(g("max_turned"), b + 1)
            chain(nc.vector.reduce_max(SM[0:8, 8:9], bank(bk)[0:8, 0:P], AX.X))
            nc.vector.tensor_scalar(SM[0:8, 16:24], CONST[0:8, C_ID:C_ID + 8], SM[0:8, 8:9], None,
                                    ALU.mult).then_inc(g("max_diag"), 1)
            dve.wait_ge(g("max_spread"), b + 1)
            chain(nc.vector.tensor_scalar(SM[:, 8:16], bank(bk)[:, P:P + 8], float(D_MODEL), None, ALU.mult))
            nc.vector.tensor_tensor(L[:, :, :], L[:, :, :], SM[:, 8:16].unsqueeze(1).broadcast_to([P, PAGES + 1, 8]),
                                    ALU.subtract).then_inc(g("l_centered"), 1)
            dve.wait_ge(g("l_exp"), b + 1)
            nc.vector.reduce_sum(SM[:, 24:32], L[:, 0:PAGES, :].rearrange("p n g -> p g n"), AX.X).then_inc(g("sum_part"), 1)
            dve.wait_ge(g("sum_spread"), b + 1)
            chain(nc.vector.scalar_tensor_tensor(out=SM[:, 0:8], in0=bank(bk)[:, P + 8:P + 16], scalar=float(D_MODEL),
                                                 in1=L[:, PAGES, :], op0=ALU.mult, op1=ALU.add))
            chain(nc.vector.reciprocal(SM[:, 8:16], SM[:, 0:8]))
            chain(nc.vector.tensor_scalar(SM[:, 9:16:2], SM[:, 9:16:2], LAM[:, 4:5], None, ALU.mult))
            chain(nc.vector.tensor_tensor(L[:, :, :], L[:, :, :], SM[:, 8:16].unsqueeze(1).broadcast_to([P, PAGES + 1, 8]),
                                          ALU.mult))
            nc.vector.tensor_tensor(AD[:, :, :], L[:, :, 0:8:2], L[:, :, 1:8:2], ALU.add).then_inc(g("weights_d"), 1)

        def decode_softmax_scalar(act, b):
            act.wait_ge(g("l_centered"), b + 1)
            nc.scalar.activation(L[:, :, :], L[:, :, :], ACT.Exp, scale=SCALE).then_inc(g("l_exp"), 1)

        def decode_softmax_tensor(pe, b, bk):
            pe.wait_ge(g("max_part"), b + 1)
            nc.tensor.transpose(bank(bk)[0:8, 0:P], SM[:, 0:8], const(C_ID)).then_inc(g("max_turned"), 1)
            pe.wait_ge(g("max_diag"), b + 1)
            nc.tensor.matmul(bank(bk)[:, P:P + 8], MEAN[0:8, :], SM[0:8, 16:24], start=True, stop=True)\
                .then_inc(g("max_spread"), 1)
            pe.wait_ge(g("sum_part"), b + 1)
            nc.tensor.matmul(bank(bk)[:, P + 8:P + 16], MEAN[:, :], SM[:, 24:32], start=True, stop=True)\
                .then_inc(g("sum_spread"), 1)

        def decode_values_tensor(pe, b, bk):
            pe.wait_ge(g("weights_d"), b + 1)
            for n in range(PAGES):
                pe.wait_ge(g(f"v_in{n % VS}"), b * (16 * PAGES // VS) + 16 * (n // VS + 1))
                for h in range(DA_HEADS):
                    mm = nc.tensor.matmul(bank(bk)[:, h:h + 1], VP[:, n % VS, P * h:P * h + P], AD[:, n, h:h + 1],
                                          start=n == 0 and h == 0, stop=n == PAGES - 1, skip_group_check=True)
                mm.then_inc(g("v_used"), 1)

        def decode_values_vector(dve, b, bk, chain):
            chain(nc.vector.tensor_tensor(SM[:, 0:4].unsqueeze(2), PROJ[:, 8:12, bass.ds(b + SEQ, 1)],
                                          AD[:, PAGES, :].unsqueeze(2), ALU.mult))
            dve.wait_ge(g("v_used"), b * PAGES + PAGES)
            nc.vector.tensor_tensor(Y[:, 0:4, bass.ds(b + SEQ, 1)], SM[:, 0:4].unsqueeze(2),
                                    bank(bk)[:, 0:4].unsqueeze(2), ALU.add).then_inc(g("d_out"), 1)

        QS, KSB, VSB, VT = U[:, 0, 0:SEQ], U[:, 1, 0:SEQ], U[:, 2, 0:SEQ], U[:, 3, 0:SEQ]
        PR = (U[:, 4, 0:SEQ], U[:, 5, 0:SEQ])
        AW = U[:, 6, 0:SEQ]
        AT = U[:, 7:11, 0:SEQ]
        QT_TILES = SEQ // P

        def logits_bank(qt, m):
            return (2 * qt + m) % 4

        def attention_pool(pool, i):
            pool.tensor_copy(QS, pj(i)[:, 0:SEQ])
            pool.tensor_copy(KSB, pj(i + 4)[:, 0:SEQ])
            pool.tensor_copy(VSB, pj(i + 8)[:, 0:SEQ]).then_inc(g("head_copied"), 1)

        def attention_tensor(pe, i):
            pe.wait_ge(g("head_copied"), i + 1)
            for t in range(QT_TILES):
                mm = nc.tensor.transpose(bank(6)[:, P * t:P * t + P], VSB[:, P * t:P * t + P], const(C_ID))
            mm.then_inc(g("v_turned"), 1)

            def logits(qt):
                for m in range(2):
                    if qt >= 2:
                        pe.wait_ge(g("exped"), i * 8 + (2 * (qt - 2) + m + 1))
                    out = bank(logits_bank(qt, m))
                    rows = slice(64 * m, 64 * m + 64)
                    nc.tensor.matmul(out[:, 0:P * (qt + 1)], QS[rows, P * qt:P * qt + P], KSB[rows, 0:P * (qt + 1)],
                                     start=True, stop=False)
                    nc.tensor.matmul(out[:, P * qt:P * qt + P], const(C_ID), const(C_CAUSAL), start=False,
                                     stop=True).then_inc(g("logits"), 1)

            logits(0)
            for qt in range(QT_TILES):
                if qt + 1 < QT_TILES:
                    logits(qt + 1)
                pe.wait_ge(g("weights_p"), i * 4 + (qt + 1))
                if qt >= 2:
                    pe.wait_ge(g("at_copied"), i * 4 + (qt - 1))
                for kb in range(qt + 1):
                    mm = nc.tensor.transpose(bank(4 + qt % 2)[:, P * kb:P * kb + P], AW[:, P * kb:P * kb + P], const(C_ID))
                mm.then_inc(g("aw_turned"), 1)
            pe.wait_ge(g("at_copied"), i * 4 + 4)
            pe.wait_ge(g("vt_copied"), i + 1)
            for kb in range(QT_TILES):
                mm = nc.tensor.matmul(bank(6)[:, P * kb:SEQ], VT[:, P * kb:P * kb + P], AT[:, kb, P * kb:SEQ],
                                      start=kb == 0, stop=kb == QT_TILES - 1)
            mm.then_inc(g("pv_done"), 1)

        def attention_scalar(act, i):
            act.wait_ge(g("v_turned"), i + 1)
            nc.scalar.activation(VT, bank(6), ACT.Copy).then_inc(g("vt_copied"), 1)
            for qt in range(QT_TILES):
                for m in range(2):
                    act.wait_ge(g("max_neg"), i * 8 + (2 * qt + m + 1))
                    if qt >= 1:
                        act.wait_ge(g("weights_p"), i * 4 + qt)
                    nc.scalar.activation(PR[m][:, 0:P * (qt + 1)], bank(logits_bank(qt, m))[:, 0:P * (qt + 1)], ACT.Exp,
                                         bias=SMP[:, 2 + m:3 + m], scale=SCALE,
                                         accum_out=SMP[:, 4 + m:5 + m]).then_inc(g("exped"), 1)
                act.wait_ge(g("aw_turned"), i * 4 + (qt + 1))
                nc.scalar.activation(AT[:, 0:qt + 1, P * qt:P * qt + P],
                                     bank(4 + qt % 2)[:, 0:P * (qt + 1)].rearrange("p (k q) -> p k q", q=P),
                                     ACT.Copy).then_inc(g("at_copied"), 1)
            act.wait_ge(g("pv_done"), i + 1)
            nc.scalar.activation(Y[:, bass.ds(i, 1), 0:SEQ].rearrange("p a n -> p (a n)"), bank(6), ACT.Copy)\
                .then_inc(g("head_out"), 1)

        def attention_vector(dve, i, chain, between):
            for qt in range(QT_TILES):
                for m in range(2):
                    dve.wait_ge(g("logits"), i * 8 + (2 * qt + m + 1))
                    chain(nc.vector.reduce_max(SMP[:, m:m + 1], bank(logits_bank(qt, m))[:, 0:P * (qt + 1)], AX.X))
                    nc.vector.tensor_scalar(SMP[:, 2 + m:3 + m], SMP[:, m:m + 1], -SCALE, None,
                                            ALU.mult).then_inc(g("max_neg"), 1)
                dve.wait_ge(g("exped"), i * 8 + (2 * qt + 2))
                chain(nc.vector.reciprocal(SMP[:, 6:8], SMP[:, 4:6]))
                chain(nc.vector.tensor_scalar(SMP[:, 7:8], SMP[:, 7:8], LAM[:, 4:5], None, ALU.mult))
                w = P * (qt + 1)
                if qt >= 1:
                    dve.wait_ge(g("aw_turned"), i * 4 + qt)
                chain(nc.vector.tensor_scalar(AW[:, 0:w], PR[0][:, 0:w], SMP[:, 6:7], None, ALU.mult))
                nc.vector.scalar_tensor_tensor(out=AW[:, 0:w], in0=PR[1][:, 0:w], scalar=SMP[:, 7:8], in1=AW[:, 0:w],
                                               op0=ALU.mult, op1=ALU.add).then_inc(g("weights_p"), 1)
                between(qt)

        XR, XK, XV, LW, AG, GG, KK, K2, BB, BO, T1 = (U[:, n, :] for n in range(11))
        CUM, DD, E1, E2, E3, OT = (SCR[:, n, :] for n in (0, 1, 2, 3, 4, 0))
        A_, B_, K_, R_, V_ = range(5)
        JOBS = []
        for q in range(2):
            JOBS += [((n, q), "v") for n in ("TT", "T", "MT", "RBT", "RKT")]
        for q in range(2):
            JOBS += [((n, q), "s") for n in ("tokB", "tokK", "tokV")]
        for n in LEVELS[1:]:
            JOBS += [(("Y", n, q), "s") for q in range(2)]
            JOBS += [((z, n, q), "v") for q in range(2) for z in (("Z", "ZT") if n != LEVELS[-1] else ("ZT",))]
        for n in range(NCH):
            if n % 4 == 0:
                JOBS += [(("O", n // 4), "v")]
            JOBS += [(("U", n), "v"), (("SA", n), "s"), (("S", n), "v")]
        RING = [name for name, _ in JOBS if name[0] != "O"]
        RING_INDEX = {name: n for n, name in enumerate(RING)}
        READER = dict(JOBS)
        READS = {}
        for e in "vs":
            for n, name in enumerate(x for x in RING if READER[x] == e):
                READS[name] = n + 1
        RING_READS = {e: sum(READER[x] == e for x in RING) for e in "vs"}

        def ring_bank(name):
            return bank(RING_INDEX[name] % 5)

        def ring_free(pe, i, name):
            n = RING_INDEX[name]
            if n >= 5:
                e = READER[RING[n - 5]]
                pe.wait_ge(g("bank_read_" + e), i * RING_READS[e] + READS[RING[n - 5]])

        def ring_full(pe, mm, name):
            mm.then_inc(g("bank_full"), 1)

        def take(eng, i, name):
            eng.wait_ge(g("bank_full"), i * len(RING) + (RING_INDEX[name] + 1))
            return ring_bank(name)

        def taken(i, name):
            return i * RING_READS[READER[name]] + READS[name]

        def quad(t, q):
            return t[:, 4 * q:4 * q + 4, :]

        def blocks(bk):
            return bk.rearrange("p (c n) -> p c n", n=P)

        def masked(c):
            return const(c).unsqueeze(1).broadcast_to([P, 4, P])

        def features_vector(dve, i, chain):
            dve.wait_ge(g("head_out"), i + 1)
            chain(nc.vector.tensor_copy(PV[:, :], VEC[:, bass.ds(i * 10 + V_PAIR, 10)]))
            w0, a0, kk, ka, rk, lg, lb, mr, mk, mv = (PV[:, n:n + 1] for n in range(10))
            for n, (x, mu) in enumerate(((XR, mr), (XK, mk), (XV, mv))):
                last = SHIFT[:, bass.ds(i + 4 * n, 1), :].rearrange("p a n -> p (a n)")
                ins = shift(dve, chain, x, i + (12 + 4 * n), last, mu)
                chain(ins)
            chain(nc.vector.tensor_scalar(KK, XK, kk, None, ALU.mult))
            nc.vector.tensor_tensor(T1, KK, KK, ALU.mult).then_inc(g("kk_squared"), 1)
            dve.wait_ge(g("gates"), i + 1)
            chain(nc.vector.tensor_scalar(LW, LW, -math.exp(-0.5), None, ALU.mult))
            chain(nc.vector.tensor_tensor_scan(CUM[:, 0:SEQ], const(C_KEEP, SEQ), LW[:, 0:SEQ], 0.0,
                                               ALU.mult, ALU.add))
            cum = CUM[:, 0:SEQ].rearrange("p (c n) -> p c n", n=CH)
            dd = DD[:, 0:SEQ].rearrange("p (c n) -> p c n", n=CH)
            chain(nc.vector.tensor_tensor(dd, cum, cum[:, :, CH // 2 - 1:CH // 2].broadcast_to([P, NCH, CH]), ALU.subtract))
            nc.vector.tensor_tensor(GAIN[:, 0:NCH - 1].unsqueeze(2), dd[:, 0:NCH - 1, CH - 1:CH],
                                    cum[:, 1:NCH, CH // 2 - 1:CH // 2], ALU.add)
            nc.vector.tensor_copy(GAIN[:, NCH - 1:NCH].unsqueeze(2), dd[:, NCH - 1:NCH, CH - 1:CH])
            nc.vector.tensor_tensor(E3[:, 0:SEQ], DD[:, 0:SEQ], LW[:, 0:SEQ], ALU.subtract).then_inc(g("exponents"), 1)
            chain(nc.vector.tensor_scalar(K2, AG, 1.0, ka, ALU.subtract, ALU.mult))
            chain(nc.vector.scalar_tensor_tensor(out=K2, in0=K2, scalar=1.0, in1=XK, op0=ALU.add, op1=ALU.mult))
            nc.vector.scalar_tensor_tensor(out=BO, in0=XR, scalar=rk, in1=K2, op0=ALU.mult,
                                           op1=ALU.mult).then_inc(g("rk_ready"), 1)
            dve.wait_ge(g("kk_norm"), i + 1)
            chain(nc.vector.tensor_scalar(T1, T1, 1e-12, None, ALU.max))
            chain(nc.vector.reciprocal(T1, T1))
            chain(nc.vector.tensor_tensor(KK, KK, T1, ALU.mult))
            chain(nc.vector.tensor_tensor(BB, KK, AG, ALU.mult))
            dve.wait_ge(g("decays"), i + 1)
            for n, (x, e) in enumerate(((KK, E3), (BB, E2), (K2, E2), (XR, E1))):
                for h in range(2):
                    rows = slice(64 * h, 64 * h + 64)
                    ins = nc.vector.tensor_tensor(BD[n][rows, :, 64 * h:64 * h + 64],
                                                  x[rows, 0:SEQ].rearrange("p (c n) -> p c n", n=CH),
                                                  e[rows, 0:SEQ].rearrange("p (c n) -> p c n", n=CH), ALU.mult)
            for h in range(2):
                rows = slice(64 * h, 64 * h + 64)
                ins = nc.vector.tensor_copy(BD[V_][rows, :, 64 * h:64 * h + 64],
                                            XV[rows, 0:SEQ].rearrange("p (c n) -> p c n", n=CH))
            ins.then_inc(g("bd_ready"), 1)
            dve.wait_ge(g("rk_summed"), i + 1)
            nc.vector.tensor_tensor(halves(BO), accv(0), halves(XV), ALU.mult).then_inc(g("bonus"), 1)

        def features_scalar(act, i):
            act.wait_ge(g("lora_done"), i + 1)
            nc.scalar.activation(PVS[:, :], VEC[:, bass.ds(i * 10 + V_PAIR, 10)], ACT.Copy).then_inc(g("pair_vectors"), 1)
            act.wait_ge(g("pair_vectors"), i + 1)
            nc.scalar.activation(halves(LW), accv(0), ACT.Sigmoid, bias=PVS[:, 0:1])
            nc.scalar.activation(halves(AG), accv(1), ACT.Sigmoid, bias=PVS[:, 1:2]).then_inc(g("gates"), 1)
            nc.scalar.activation(halves(GG), accv(2), ACT.Copy).then_inc(g("g_ready"), 1)
            act.wait_ge(g("kk_summed"), i + 1)
            nc.scalar.activation(halves(T1), accv(0), ACT.Sqrt).then_inc(g("kk_norm"), 1)
            act.wait_ge(g("exponents"), i + 1)
            nc.scalar.activation(E1[:, 0:SEQ], DD[:, 0:SEQ], ACT.Exp)
            nc.scalar.activation(E2[:, 0:SEQ], DD[:, 0:SEQ], ACT.Exp, scale=-1.0)
            nc.scalar.activation(GAIN[:, :], GAIN[:, :], ACT.Exp)
            nc.scalar.activation(E3[:, 0:SEQ], E3[:, 0:SEQ], ACT.Exp).then_inc(g("decays"), 1)

        def features_tensor(pe, i):
            pe.wait_ge(g("lora_in_sbuf"), i * 32 + 32)
            pe.wait_ge(g("lora_act"), 1)
            pe.wait_ge(g("head_out"), i + 1)
            for a in range(2):
                cols = slice(HALF * a, HALF * a + HALF)
                nc.tensor.matmul(acc[0][:, a, 0:HALF], LORA[0:64, :], XWA[0:64, cols], start=True, stop=True)
                nc.tensor.matmul(acc[1][:, a, 0:HALF], LORA[64:P, :], XWA[64:P, cols], start=True, stop=True)
                mm = nc.tensor.matmul(acc[2][:, a, 0:HALF], LG2[:, :], XSG[:, cols], start=True, stop=True)
            mm.then_inc(g("lora_done"), 1)
            pe.wait_ge(g("kk_squared"), i + 1)
            pe.wait_ge(g("gates"), i + 1)
            for a in range(2):
                mm = nc.tensor.matmul(acc[0][:, a, 0:HALF], const(C_HEAD), T1[:, HALF * a:HALF * a + HALF], start=True, stop=True)
            mm.then_inc(g("kk_summed"), 1)
            pe.wait_ge(g("kk_norm"), i + 1)
            pe.wait_ge(g("rk_ready"), i + 1)
            for a in range(2):
                mm = nc.tensor.matmul(acc[0][:, a, 0:HALF], const(C_HEAD), BO[:, HALF * a:HALF * a + HALF], start=True, stop=True)
            mm.then_inc(g("rk_summed"), 1)

        def chunks_tensor(pe, i):
            pe.wait_ge(g("bonus"), i + 1)
            pe.wait_ge(g("g_ready"), i + 1)
            pe.wait_ge(g("bd_ready"), i + 1)

            def products(name, q, lhs, rhs):
                ring_free(pe, i, name)
                for c in range(4):
                    mm = nc.tensor.matmul(ring_bank(name)[:, P * c:P * c + P], lhs(c), rhs(c), start=True, stop=True)
                ring_full(pe, mm, name)

            bd = lambda n, q: (lambda c: BD[n][:, 4 * q + c, :])
            for q in range(2):
                for name, a, b in (("TT", B_, A_), ("T", A_, B_), ("MT", K_, A_), ("RBT", B_, R_), ("RKT", K_, R_)):
                    products((name, q), q, bd(a, q), bd(b, q))
            for q in range(2):
                for name, n in (("tokB", B_), ("tokK", K_), ("tokV", V_)):
                    ring_free(pe, i, (name, q))
                    for c in range(4):
                        mm = nc.tensor.transpose(ring_bank((name, q))[:, P * c:P * c + P], BD[n][:, 4 * q + c, :], const(C_ID))
                    ring_full(pe, mm, (name, q))
            of = lambda t, q: (lambda c: t[:, 4 * q + c, :])
            for l, n in enumerate(LEVELS[1:]):
                for q in range(2):
                    pe.wait_ge(g("level_masked"), i * 10 + (2 * l + q + 1))
                    pe.wait_ge(g("bank_read_v"), taken(i, ("ZT", LEVELS[l], q)) if l else taken(i, ("T", q)))
                    products(("Y", n, q), q, of(EE, q), of(PP, q))
                for q in range(2):
                    pe.wait_ge(g("bank_read_s"), taken(i, ("Y", n, q)))
                    if n != LEVELS[-1]:
                        products(("Z", n, q), q, of(PT, q), of(YY, q))
                    products(("ZT", n, q), q, of(YY, q), of(PT, q))
            for n in range(NCH):
                q, c = n // 4, n % 4
                if n == 0:
                    pe.wait_ge(g("bank_read_s"), taken(i, ("tokV", 1)))
                    pe.wait_ge(g("bank_read_v"), taken(i, ("ZT", LEVELS[-1], 1)))
                name = ("U", n)
                ring_free(pe, i, name)
                mm = nc.tensor.matmul(ring_bank(name)[:, 0:P], MT[:, n, :], TK[V_][:, n, :], start=True, stop=n == 0)
                if n:
                    pe.wait_ge(g("bank_read_v"), taken(i, ("S", n - 1)))
                    mm = nc.tensor.matmul(ring_bank(name)[:, 0:P], BD[A_][:, n, :], ST[:, n % 2, :], start=False, stop=True)
                ring_full(pe, mm, name)
                if c == 0:
                    if q == 1:
                        pe.wait_ge(g("out_read"), i * 2 + 1)
                ob = bank(5)[:, P * c:P * c + P]
                nc.tensor.matmul(ob, TK[V_][:, n, :], RKT[:, n, :], start=True, stop=False)
                if n:
                    nc.tensor.matmul(ob, ST[:, n % 2, :], BD[R_][:, n, :], start=False, stop=False)
                pe.wait_ge(g("bank_read_v"), taken(i, ("U", n)))
                name = ("SA", n)
                ring_free(pe, i, name)
                mm = nc.tensor.matmul(ring_bank(name)[:, 0:P], PT[:, n, :], UN[:, :], start=True, stop=True)
                ring_full(pe, mm, name)
                name = ("S", n)
                ring_free(pe, i, name)
                nc.tensor.matmul(ring_bank(name)[:, 0:P], TK[K_][:, n, :], TK[V_][:, n, :], start=True, stop=False)
                pe.wait_ge(g("bank_read_s"), taken(i, ("SA", n)))
                mm = nc.tensor.matmul(ring_bank(name)[:, 0:P], TK[B_][:, n, :], SA[:, :], start=False, stop=True)
                ring_full(pe, mm, name)
                mm = nc.tensor.matmul(ob, SA[:, :], RBT[:, n, :], start=False, stop=True)
                mm.then_inc(g("out_chunk"), 1)

        def chunks_vector(dve, i, chain, between):
            for q in range(2):
                for name, out, mask in ((("TT", q), TT, C_STRICT), (("T", q), None, None), (("MT", q), MT, C_STRICT),
                                        (("RBT", q), RBT, C_INCL), (("RKT", q), RKT, C_INCL)):
                    src = blocks(take(dve, i, name))
                    if out is None:
                        chain(nc.vector.tensor_tensor(quad(PP, q), src, masked(C_LOW1), ALU.mult))
                        ins = nc.vector.tensor_tensor(quad(PP, q), masked(C_ID), quad(PP, q), ALU.subtract)
                    else:
                        ins = nc.vector.tensor_tensor(quad(out, q), src, masked(mask), ALU.mult)
                    ins.then_inc(g("bank_read_v"), 1)
                    if out is TT:
                        dve.wait_ge(g("bank_read_v"), taken(i, name))
                        chain(nc.vector.tensor_tensor(quad(PT, q), quad(TT, q), masked(C_LEV), ALU.mult))
                        chain(nc.vector.tensor_tensor(quad(PT, q), masked(C_ID), quad(PT, q), ALU.subtract))
            for l, n in enumerate(LEVELS[1:]):
                between(l)
                for q in range(2):
                    for z, t in (("Z", PP), ("ZT", PT)):
                        if (z, n, q) in RING_INDEX:
                            src = blocks(take(dve, i, (z, n, q)))
                            if z == "Z":
                                dve.wait_ge(g("bank_full"), i * len(RING) + (RING_INDEX[("ZT", n, q)] + 1))
                            nc.vector.tensor_tensor(quad(t, q), quad(t, q), src, ALU.subtract).then_inc(g("bank_read_v"), 1)
            chain(nc.vector.memset(SG[:, :], 0.0))
            for n in range(NCH):
                src = take(dve, i, ("U", n))[:, 0:P]
                nc.vector.tensor_scalar(UN[:, :], src, -1.0, None, ALU.mult).then_inc(g("bank_read_v"), 1)
                if n:
                    chain(nc.vector.tensor_scalar(SG[:, :], ST[:, n % 2, :], GAIN[:, n:n + 1], None, ALU.mult))
                src = take(dve, i, ("S", n))[:, 0:P]
                if n:
                    dve.wait_ge(g("out_chunk"), i * NCH + n)
                nc.vector.scalar_tensor_tensor(out=ST[:, (n + 1) % 2, :], in0=src, scalar=GAIN[:, n:n + 1], in1=SG[:, :],
                                               op0=ALU.mult, op1=ALU.add).then_inc(g("bank_read_v"), 1)
                dve.wait_ge(g("bank_read_v"), taken(i, ("S", n)))
                if n % 4 == 3:
                    dve.wait_ge(g("out_chunk"), i * NCH + (n + 1))
                    for h in range(2):
                        rows = slice(64 * h, 64 * h + 64)
                        ins = nc.vector.tensor_copy(OT[rows, CH * (n - 3):CH * (n + 1)].rearrange("p (c n) -> p c n", n=CH),
                                                    blocks(bank(5))[rows, :, 64 * h:64 * h + 64])
                    ins.then_inc(g("out_read"), 1)

        def chunks_scalar(act, i):
            for q in range(2):
                for name, n in (("tokB", B_), ("tokK", K_), ("tokV", V_)):
                    src = blocks(take(act, i, (name, q)))
                    nc.scalar.activation(quad(TK[n], q), src, ACT.Copy).then_inc(g("bank_read_s"), 1)
            for n in LEVELS[1:]:
                for q in range(2):
                    src = blocks(take(act, i, ("Y", n, q)))
                    if n > 2:
                        act.wait_ge(g("bank_full"), i * len(RING) + (RING_INDEX[("ZT", n // 2, q)] + 1))
                    nc.scalar.activation(quad(YY, q), src, ACT.Copy).then_inc(g("bank_read_s"), 1)
            for n in range(NCH):
                src = take(act, i, ("SA", n))[:, 0:P]
                if n:
                    act.wait_ge(g("out_chunk"), i * NCH + n)
                nc.scalar.activation(SA[:, :], src, ACT.Copy).then_inc(g("bank_read_s"), 1)

        def levels_pool(pool, i, between):
            for l, n in enumerate(LEVELS[1:]):
                between(l)
                for q in range(2):
                    if l == 0:
                        pool.wait_ge(g("bank_read_v"), taken(i, ("TT", q)))
                    else:
                        pool.wait_ge(g("bank_full"), i * len(RING) + (RING_INDEX[("Y", n // 2, q)] + 1))
                    pool.tensor_tensor(quad(EE, q), quad(TT, q), masked(C_LEV + P * (l + 1)), ALU.mult)\
                        .then_inc(g("level_masked"), 1)

        def step_vector(dve, i, chain):
            s3 = lambda t: t.rearrange("p (b v) -> p b v", v=64)
            SS, PD, VB = SCR[:, 1, 0:SEQ], SCR[:, 2, 0:SEQ], SCR[:, 3, 0:SEQ]

            def per_key(x):
                return x[:, SEQ:TOK].unsqueeze(2).broadcast_to([P, DEC, 64])
            dve.wait_ge(g("state_in"), i * 16 + 16)
            chain(nc.vector.tensor_tensor(s3(PD), s3(SS), per_key(KK), ALU.mult))
            nc.vector.tensor_tensor(s3(VB), ID2[:, :].unsqueeze(1).broadcast_to([P, DEC, 64]), per_key(XV),
                                    ALU.mult).then_inc(g("step_terms"), 1)
            dve.wait_ge(g("decay_d"), i + 1)
            chain(nc.vector.tensor_tensor(s3(SS), s3(SS), per_key(T1), ALU.mult))
            dve.wait_ge(g("step_sums"), i + 1)
            chain(nc.vector.tensor_tensor(s3(PD), s3(bank(6)), per_key(BB), ALU.mult))
            chain(nc.vector.tensor_tensor(SS, SS, PD, ALU.subtract))
            chain(nc.vector.tensor_tensor(s3(VB), s3(bank(5)), per_key(K2), ALU.mult))
            nc.vector.tensor_tensor(SS, SS, VB, ALU.add).then_inc(g("step_state"), 1)
            dve.wait_ge(g("step_state"), i + 1)
            nc.vector.tensor_tensor(s3(PD), s3(SS), per_key(XR), ALU.mult).then_inc(g("step_read"), 1)
            dve.wait_ge(g("step_out"), i + 1)
            chain(nc.vector.tensor_tensor(s3(VB), s3(bank(6)), ID2[:, :].unsqueeze(1).broadcast_to([P, DEC, 64]), ALU.mult))
            nc.vector.reduce_sum(OT[:, SEQ:TOK], s3(VB), AX.X).then_inc(g("o_ready"), 1)

        def step_tensor(pe, i):
            SS, PD, VB = SCR[:, 1, 0:SEQ], SCR[:, 2, 0:SEQ], SCR[:, 3, 0:SEQ]
            pe.wait_ge(g("step_terms"), i + 1)
            pe.wait_ge(g("out_read"), i * 2 + 2)
            nc.tensor.matmul(bank(6), const(C_HEAD), PD, start=True, stop=True)
            nc.tensor.matmul(bank(5), const(C_HEAD), VB, start=True, stop=True).then_inc(g("step_sums"), 1)
            pe.wait_ge(g("step_read"), i + 1)
            nc.tensor.matmul(bank(6), const(C_HEAD), PD, start=True, stop=True).then_inc(g("step_out"), 1)

        def step_scalar(act, i):
            act.wait_ge(g("bd_ready"), i + 1)
            act.dma_start(SCR[:, 1, 0:SEQ], state_in[bass.ds(i, 1), :, :].rearrange("a p n -> (a p) n"))\
                .then_inc(g("state_in"), 16)
            nc.scalar.activation(T1[:, SEQ:TOK], LW[:, SEQ:TOK], ACT.Exp).then_inc(g("decay_d"), 1)

        def output_vector(dve, i, chain):
            dve.wait_ge(g("gn_mean"), i + 1)
            chain(nc.vector.scalar_tensor_tensor(out=halves(OT), in0=accv(0), scalar=-1.0 / 64, in1=halves(OT),
                                                 op0=ALU.mult, op1=ALU.add))
            nc.vector.tensor_tensor(T1, OT, OT, ALU.mult).then_inc(g("gn_squared"), 1)
            dve.wait_ge(g("gn_std"), i + 1)
            chain(nc.vector.reciprocal(T1, T1))
            chain(nc.vector.tensor_tensor(OT, OT, T1, ALU.mult))
            chain(nc.vector.tensor_scalar(OT, OT, PV[:, 5:6], PV[:, 6:7], ALU.mult, ALU.add))
            chain(nc.vector.tensor_tensor(OT, OT, BO, ALU.add))
            nc.vector.tensor_tensor(Y[:, bass.ds(i + 4, 1), :].rearrange("p a n -> p (a n)"), OT, GG,
                                    ALU.mult).then_inc(g("turn_done"), 1)

        def output_tensor(pe, i):
            pe.wait_ge(g("o_ready"), i + 1)
            for a in range(2):
                mm = nc.tensor.matmul(acc[0][:, a, 0:HALF], const(C_HEAD), OT[:, HALF * a:HALF * a + HALF], start=True, stop=True)
            mm.then_inc(g("gn_mean"), 1)
            pe.wait_ge(g("gn_squared"), i + 1)
            for a in range(2):
                mm = nc.tensor.matmul(acc[1][:, a, 0:HALF], const(C_HEAD), T1[:, HALF * a:HALF * a + HALF], start=True, stop=True)
            mm.then_inc(g("gn_var"), 1)

        def output_scalar(act, i):
            act.wait_ge(g("gn_var"), i + 1)
            nc.scalar.activation(halves(T1), accv(1), ACT.Sqrt, bias=EPS[:, 3:4], scale=1.0 / 64).then_inc(g("gn_std"), 1)

        D_BANK = 7
        PAGES_AT = [range(4 * n, 4 * n + 4) for n in range(4)] + [range(0)]
        LINKS = 78

        def turn_pool(pool, i):
            attention_pool(pool, i)
            decode_query_pool(pool, 2 * i)
            decode_pages_pool(pool, 2 * i, range(PAGES))
            decode_query_pool(pool, 2 * i + 1)
            levels_pool(pool, i, lambda l: decode_pages_pool(pool, 2 * i + 1, PAGES_AT[l]))
            pool.wait_ge(g("turn_done"), i + 1)

        def turn_tensor(pe, i):
            decode_query_tensor(pe, 2 * i, D_BANK)
            attention_tensor(pe, i)
            decode_softmax_tensor(pe, 2 * i, D_BANK)
            features_tensor(pe, i)
            decode_values_tensor(pe, 2 * i, D_BANK)
            decode_query_tensor(pe, 2 * i + 1, D_BANK)
            chunks_tensor(pe, i)
            decode_softmax_tensor(pe, 2 * i + 1, D_BANK)
            step_tensor(pe, i)
            decode_values_tensor(pe, 2 * i + 1, D_BANK)
            output_tensor(pe, i)
            pe.wait_ge(g("turn_done"), i + 1)

        def turn_scalar(act, i):
            act.dma_start(LORA[:, :], lora[bass.ds(i, 1), :, :].rearrange("a p n -> (a p) n")).then_inc(g("lora_in_sbuf"), 16)
            act.dma_start(LG2[:, :], g2[bass.ds(i, 1), :, :].rearrange("a p n -> (a p) n")).then_inc(g("lora_in_sbuf"), 16)
            decode_query_scalar(act, 2 * i, D_BANK)
            attention_scalar(act, i)
            decode_softmax_scalar(act, 2 * i)
            features_scalar(act, i)
            step_scalar(act, i)
            decode_query_scalar(act, 2 * i + 1, D_BANK)
            chunks_scalar(act, i)
            act.wait_ge(g("bank_read_v"), taken(i, ("S", NCH - 1)))
            act.dma_start(wkv_out[bass.ds(i, 1), :, :].rearrange("a p n -> (a p) n"), ST[:, 0, :]).then_inc(g("states_out"), 16)
            decode_softmax_scalar(act, 2 * i + 1)
            act.wait_ge(g("step_state"), i + 1)
            act.dma_start(wkv_s_out[bass.ds(i, 1), :, :].rearrange("a p n -> (a p) n"), SCR[:, 1, 0:SEQ]).then_inc(g("states_out"), 16)
            output_scalar(act, i)
            act.wait_ge(g("states_out"), i * 32 + 32)
            act.wait_ge(g("turn_done"), i + 1)

        def turn_vector(dve, i):
            chain = Chain(dve, g("dve_turn"), i, LINKS)
            b = 2 * i
            attention_vector(dve, i, chain, lambda qt: decode_pages_vector(dve, b, PAGES_AT[qt]))
            decode_softmax_vector(dve, b, D_BANK, chain)
            features_vector(dve, i, chain)
            decode_values_vector(dve, b, D_BANK, chain)
            chunks_vector(dve, i, chain, lambda l: decode_pages_vector(dve, b + 1, PAGES_AT[l]))
            decode_softmax_vector(dve, b + 1, D_BANK, chain)
            step_vector(dve, i, chain)
            decode_values_vector(dve, b + 1, D_BANK, chain)
            output_vector(dve, i, chain)
            chain.end()

        def mixed_scalar(act):
            act.wait_ge(g("turn_done"), DA_HEADS)
            act.wait_ge(stored, 3 * 16)
            for c in range(DA_HEADS):
                nc.scalar.activation(SCR[:, c, :], Y[:, c, :], ACT.Square).then_inc(g("m_squared"), 1)
            for c in range(DA_HEADS, DC):
                nc.scalar.activation(MH[:, c, :], Y[:, c, :], ACT.Copy).then_inc(g("mix_hi"), 1)
            for c in range(DA_HEADS):
                act.wait_ge(g("m_summed"), c + 1)
                nc.scalar.activation(halves(SCR[:, c, :]), accv(c), ACT.Sqrt, bias=EPS[:, 4:5],
                                     scale=float(D_MODEL // P)).then_inc(g("m_std"), 1)
            for c in range(DA_HEADS):
                act.wait_ge(g("m_scaled"), c + 1)
                nc.scalar.activation(MH[:, c, :], Y[:, c, :], ACT.Copy).then_inc(g("mix_hi"), 1)

        def mixed_tensor(pe):
            for c in range(DA_HEADS):
                pe.wait_ge(g("m_squared"), c + 1)
                for a in range(2):
                    mm = nc.tensor.matmul(acc[c][:, a, 0:HALF], MEAN[:, :], SCR[:, c, HALF * a:HALF * a + HALF],
                                          start=True, stop=True)
                mm.then_inc(g("m_summed"), 1)

        def mixed_vector(dve):
            chain = Chain(dve, g("dve_mixed"))
            chain(nc.vector.tensor_scalar(VEC[:, V_SUB:V_SUB + 1], VEC[:, V_SUB:V_SUB + 1], 1.0 - LAM_INIT, None, ALU.mult))
            order = list(range(DA_HEADS, DC)) + list(range(DA_HEADS))
            for n, c in enumerate(order):
                if c < DA_HEADS:
                    dve.wait_ge(g("m_std"), c + 1)
                    chain(nc.vector.reciprocal(SCR[:, c, :], SCR[:, c, :]))
                    nc.vector.scalar_tensor_tensor(out=Y[:, c, :], in0=Y[:, c, :], scalar=VEC[:, V_SUB:V_SUB + 1],
                                                   in1=SCR[:, c, :], op0=ALU.mult, op1=ALU.mult).then_inc(g("m_scaled"), 1)
                dve.wait_ge(g("mix_hi"), n + 1)
                nc.vector.tensor_tensor(ML[:, c, :], Y[:, c, :], MH[:, c, :].bitcast(f32), ALU.subtract)\
                    .then_inc(g("mix_ready"), 1)

        block = ctx.enter_context(nc.Block())

        @block.sync
        def _(sp):
            sp.dma_start(Y[:, :, :], x_in).then_inc(x_loaded, 16)

            def stream(pr, src):
                load_weights(sp, pr, 0, lambda i, b: src(0, b))
                if pr.times > 1:
                    with sp.Fori(1, pr.times) as i:
                        load_weights(sp, pr, i, src)

            def by_pair(w):
                return lambda i, b: w[bass.ds(i * 2 + b, 1), :, :].rearrange("a p (k n) -> p (a k) n", n=2 * P)

            def down(w):
                def src(i, b):
                    k0, nk = DOWN_BODY[b][:2]
                    return w[bass.ds(i * 2 + b // 4, 1), :, k0 * 2 * P:(k0 + nk) * 2 * P]\
                        .rearrange("a p (k n) -> p (a k) n", n=2 * P)
                return src

            stream(up_a, by_pair(gu_a))
            stream(dn_a, down(down_a))
            stream(inp, by_pair(w_in))
            stream(inp_tail, lambda i, b: w_in[12, :, :].rearrange("p (k n) -> p k n", n=2 * P))
            sp.wait_ge(slab_used, 2 * inp.block0)
            sp.dma_start(CONST[:, :], consts[:, 0:NCONST]).then_inc(g("consts_in"), 16)
            sp.dma_start(LAMV[:, :], lams).then_inc(g("small_in"), 16)
            sp.dma_start(SHIFT[:, :, :], shift_in).then_inc(g("small_in"), 16)
            sp.dma_start(TABLE[:, :], pages).then_inc(g("table_in"), 16)
            sp.wait_ge(x_ready, 2 * DC)
            sp.dma_start(Y[:, 6:8, :], consts[:, NCONST:NCONST + 2 * TOK].rearrange("p (a n) -> p a n", n=TOK))\
                .then_inc(g("small_in"), 16)
            projected(sp)
            sp.dma_start(hi_dram, XH[:, :, :].bitcast(f32)).then_inc(g("spilled"), 16)
            sp.dma_start(lo_dram, XL[:, :, :].bitcast(f32)).then_inc(g("spilled"), 16)
            sp.dma_start(v_out, PROJ[:, 8:12, :]).then_inc(stored, 16)
            sp.dma_start(shift_out, PROJ[:, 12:IN_CHUNKS, SEQ - 1:TOK]).then_inc(stored, 16)
            sp.wait_ge(g("table_in"), 16)
            decode_loads(sp)
            sp.wait_ge(g("roped"), 8)
            sp.dma_start(k_out, PROJ[:, 4:8, :]).then_inc(stored, 16)
            sp.wait_ge(g("turn_done"), DA_HEADS)
            stream(outp, by_pair(w_out))
            sp.dma_start(XH[:, :, :].bitcast(f32), hi_dram).then_inc(g("restored"), 16)
            sp.dma_start(XL[:, :, :].bitcast(f32), lo_dram).then_inc(g("restored"), 16)
            sp.wait_ge(stored, 3 * 16)
            stream(up_b, by_pair(gu_b))
            stream(dn_b, down(down_b))
            for c in range(DC):
                sp.wait_ge(x_hi, 3 * DC + c + 1)
                sp.dma_start(y_out[:, c, :], Y[:, c, :]).then_inc(stored, 16)
            sp.wait_ge(stored, 16 * (3 + DC))

        @block.gpsimd
        def _(pool):
            pool.memset(MEAN[:, :], 1.0 / D_MODEL).then_inc(consts_set, 1)
            for n, e in enumerate((4 * LN_EPS, LN_EPS, 4 * LN_EPS, GN_EPS, LN_EPS)):
                pool.memset(EPS[:, n:n + 1], e).then_inc(consts_set, 1)
            pool.wait_ge(g("small_in"), 48)
            prelude_pool(pool)
            pool.wait_ge(g("spilled"), 32)
            for n in range(5):
                pool.memset(BD[n][:, :, :], 0.0).then_inc(g("blocks_cleared"), 1)
            with pool.Fori(0, DA_HEADS) as i:
                turn_pool(pool, i)

        @block.scalar
        def _(act):
            act.dma_start(VEC[:, :], vecs).then_inc(tables_in, 16)
            act.wait_ge(consts_set, 6)
            act.wait_ge(x_loaded, 16)
            for c in range(DC):
                nc.scalar.activation(XH[:, c, :], Y[:, c, :], ACT.Copy).then_inc(x_hi, 1)
            act.wait_ge(tables_in, 16)
            gate_up(gate_up_scalar, act, up_a, 0)
            down_scalar(act, dn_a)
            norm_scalar(act, 0)
            input_scalar(act)
            prelude_scalar(act)
            act.wait_ge(g("spilled"), 32)
            with act.Fori(0, DA_HEADS) as i:
                turn_scalar(act, i)
            mixed_scalar(act)
            for k in range(4):
                split_high(act, outp, 0, k)
            for k in range(4):
                split_high(act, outp, 1, k)
            norm_scalar(act, 1)
            gate_up(gate_up_scalar, act, up_b, 1)
            down_scalar(act, dn_b)
            norm_scalar(act, 2, out=True)

        @block.vector
        def _(dve):
            dve.wait_ge(x_loaded, 16)
            dve.wait_ge(tables_in, 16)
            for c in range(DC):
                dve.wait_ge(x_hi, c + 1)
                nc.vector.tensor_tensor(XL[:, c, :], Y[:, c, :], XH[:, c, :].bitcast(f32),
                                        ALU.subtract).then_inc(x_ready, 1)
            gate_up(gate_up_vector, dve, up_a, 0)
            down_vector(dve, dn_a)
            norm_vector(dve, 0)
            for k in range(4):
                split_low(dve, inp, 0, k)
            with dve.Fori(1, inp.times) as i:
                for k in range(4):
                    split_low(dve, inp, i, k)
            for k in range(2):
                split_low(dve, inp_tail, 0, k)
            dve.wait_ge(g("spilled"), 32)
            prelude_vector(dve)
            dve.wait_ge(g("blocks_cleared"), 5)
            with dve.Fori(0, DA_HEADS) as i:
                turn_vector(dve, i)
            mixed_vector(dve)
            for k in range(4):
                split_low(dve, outp, 0, k)
            dve.wait_ge(g("restored"), 32)
            for i in range(2):
                for k in range(4):
                    residual(dve, outp, i, k, 4 * i + k, ALPHA)
                    if i == 0:
                        split_low(dve, outp, 1, k)
            norm_vector(dve, 1)
            gate_up(gate_up_vector, dve, up_b, 1)
            down_vector(dve, dn_b)
            norm_vector(dve, 2, last=True)

        @block.tensor
        def _(pe):
            pe.wait_ge(consts_set, 6)
            gate_up_tensor(pe, up_a, 0)
            down_tensor(pe, dn_a, 0)
            norm_tensor(pe, 0)
            pe.wait_ge(x_ready, 2 * DC)
            multiply(pe, inp, 0, XH, XL)
            with pe.Fori(1, inp.times) as i:
                multiply(pe, inp, i, XH, XL)
            multiply(pe, inp_tail, 0, XH, XL)
            prelude_tensor(pe)
            pe.wait_ge(g("own_ready"), 1)
            with pe.Fori(0, DA_HEADS) as i:
                turn_tensor(pe, i)
            mixed_tensor(pe)
            pe.wait_ge(g("m_std"), DA_HEADS)
            pe.wait_ge(g("mix_ready"), DC)
            for i in range(2):
                multiply(pe, outp, i, MH, ML)
            norm_tensor(pe, 1)
            gate_up_tensor(pe, up_b, 2)
            down_tensor(pe, dn_b, 1)
            norm_tensor(pe, 2)


def constants():
    a = np.arange(P)
    t, s = a[None, :], a[:, None]
    head = t // CH == s // CH
    out = [t == s,
           (t // 64 == s // 64) & ((t % 64 + 32) % 64 == s % 64),
           np.where(s < t, NEG, 0.0),
           head & (s < t), head & (s <= t), head,
           (s % 2 == 1) & (t == s - 1)]
    for n in LEVELS:
        out.append(head & ((t // n) % 2 == 1) & (s // n == t // n - 1))
    keep = np.broadcast_to(np.arange(SEQ) % CH != 0, (P, SEQ))
    half = DA_QK // 2
    inv = np.float32(10000.0) ** (-np.arange(half, dtype=np.float32) / np.float32(half))
    pos = np.concatenate([np.arange(SEQ), np.full(DEC, PAST)]).astype(np.float32)
    ang = (pos[:, None] * inv.astype(np.float32)[None, :]).astype(np.float32).T
    cos = np.tile(np.cos(ang), (4, 1))
    sin = np.concatenate([-np.sin(ang), np.sin(ang)] * 2, 0)
    return np.concatenate([np.asarray(x, np.float32) for x in (*out, keep, cos, sin)], 1)


def kernel(**a):
    import concourse.bacc as bacc
    from concourse.bass_utils import run_bass_kernel_spmd

    def fm(v, n):
        return v.reshape(n, P).T

    x = np.concatenate([a["x_prompt"][0], a["x_sample"][:, 0]], 0).T.reshape(DC, P, TOK).transpose(1, 0, 2)

    def by_pair(w):
        return w[0].reshape(DC, P, -1, 2 * P).transpose(2, 1, 0, 3).reshape(-1, P, DC * 2 * P)

    def gate_up(w):
        return w[0].reshape(DC, P, 2, FC // 2, 2 * P).transpose(3, 2, 1, 0, 4).reshape(FC, P, DC * 2 * P)

    def down(w):
        return w[0].reshape(FC, P, DC // 2, 2 * P).transpose(2, 1, 0, 3).reshape(DC // 2, P, FC * 2 * P)

    mu = fm(a["rw_mu"], RC)
    cols = [fm(a[n], DC) for n in ("ln1_g", "ln1_b", "ln2_g", "ln2_b", "ln3_g", "ln3_b")]
    cols += [fm(a["da_subln_g"], 1), mu[:, 12:14]]
    per = [fm(a[n], 4) for n in ("rw_w0", "rw_a0", "rw_k_k", "rw_k_a", "rw_r_k", "rw_lnx_g", "rw_lnx_b")]
    for i in range(4):
        cols += [v[:, i:i + 1] for v in per] + [mu[:, i + 4 * n:i + 4 * n + 1] for n in range(3)]
    lam = np.concatenate([a[n][0] for n in ("da_lq1", "da_lk1", "da_lq2", "da_lk2")])
    lora = np.concatenate([a["rw_w2"][0], a["rw_a2"][0]], 0).reshape(P, 4, P).transpose(1, 0, 2)
    state = a["state_wkv"][0].reshape(DEC, 4, 2, 64, 64).transpose(1, 2, 4, 0, 3).reshape(4, P, DEC * 64)
    ins = {
        "x": x, "gate_up_a": gate_up(a["ffa_w_gu"]), "down_a": down(a["ffa_w_down"]), "w_in": by_pair(a["w_in"]),
        "w_out": by_pair(a["w_out"]), "gate_up_b": gate_up(a["ffb_w_gu"]), "down_b": down(a["ffb_w_down"]),
        "constants": constants(), "vectors": np.concatenate(cols, 1), "lambdas": np.broadcast_to(lam, (P, 256)),
        "lora": lora, "g2": a["rw_g2"][0].reshape(P, 4, P).transpose(1, 0, 2),
        "cache_k": a["cache_k"][0].reshape(POOL, PAGE, 512), "cache_v": a["cache_v"][0].reshape(POOL, PAGE, 512),
        "pages": a["page_table"].reshape(1, DEC * PAGES), "state": state,
        "shift": a["state_shift"][0, :, 0].T.reshape(RC, P, DEC).transpose(1, 0, 2),
    }
    ins = {k: np.ascontiguousarray(v) for k, v in ins.items()}
    outs = {"y": (P, DC, TOK), "k": (P, 4, TOK), "v": (P, 4, TOK), "wkv": (4, P, P),
            "shift_rows": (P, RC, TOK - SEQ + 1), "wkv_decode": (4, P, DEC * 64)}
    nc = bacc.Bacc("TRN2", target_bir_lowering=False, num_devices=1)
    t = [nc.dram_tensor(f"in_{n}", v.shape, mybir.dt.from_np(v.dtype), kind="ExternalInput").ap() for n, v in ins.items()]
    o = [nc.dram_tensor(f"out_{n}", s, mybir.dt.float32, kind="ExternalOutput").ap() for n, s in outs.items()]
    layer(nc, *t, *o)
    r = run_bass_kernel_spmd(nc, [{f"in_{k}": v for k, v in ins.items()}], core_ids=[0]).results[0]

    def tokens(v):
        return v.transpose(2, 1, 0).reshape(v.shape[2], -1)

    y, k, v, sh = (tokens(r[f"out_{n}"]) for n in ("y", "k", "v", "shift_rows"))
    w = r["out_wkv"].reshape(4, 2, 64, 2, 64)
    wkv = np.stack([w[:, h, :, h, :] for h in range(2)], 1).reshape(8, 64, 64).transpose(0, 2, 1)
    wkv_d = r["out_wkv_decode"].reshape(4, 2, 64, DEC, 64).transpose(3, 0, 1, 4, 2).reshape(1, DEC, 8, 64, 64)
    c = np.ascontiguousarray
    return (c(y[None, :SEQ]), c(y[SEQ:, None]), c(k[:SEQ].reshape(1, 1, SEQ, 4, P)), c(v[:SEQ].reshape(1, 1, SEQ, 4, P)),
            c(wkv[None, None]), c(sh[:1].reshape(1, 1, 1, RW_PROJ)), c(k[SEQ:].reshape(1, DEC, 1, 4, P)),
            c(v[SEQ:].reshape(1, DEC, 1, 4, P)), c(wkv_d), c(sh[1:].reshape(1, DEC, 1, RW_PROJ)))
```

```python
import math
import numpy as np
import concourse.bass as bass
from concourse import mybir
from contextlib import ExitStack

P = 128
D_MODEL, SEQ, DEC = 1024, 512, 8
TOK = SEQ + DEC
HALF = TOK // 2
DC = D_MODEL // P
D_FF = 2816
FC = D_FF // P
DA_HEADS, DA_QK = 4, 64
RW_DIM, RW_PROJ = 512, 1792
RC = RW_PROJ // P
IN_CHUNKS = 3 * DA_HEADS + RC
PAST, PAGE = 2048, 128
PAGES = PAST // PAGE
POOL = 160
ALPHA = 2 ** 0.25
LN_EPS = 1e-5
GN_EPS = 64e-5
LAM_INIT = 0.8 - 0.6 * math.exp(-0.0)
SCALE = DA_QK ** -0.5
NEG = -1e30
CH = 64
NCH = SEQ // CH
LEVELS = (1, 2, 4, 8, 16, 32)
DOWN_K = (6, 6, 5, 5)

C_ID, C_SWAP, C_CAUSAL, C_STRICT, C_INCL, C_HEAD = (P * n for n in range(6))
C_LOW1 = P * 6
C_LEV = P * 7
C_KEEP = C_LEV + P * len(LEVELS)
NCONST = C_KEEP + SEQ

V_LN = 0
V_SUB = V_LN + 6 * DC
V_MU2 = V_SUB + 1
V_PAIR = V_MU2 + 2
NVEC = V_PAIR + 40
KS, VS = 4, 4


class Product:

    def __init__(self, body, times, before=None):
        self.body, self.times = body, times
        self.block0 = before.block0 + before.times * len(before.body) if before else 0
        used = [0] * 4
        for _, _, sets, begins, _ in body:
            for s in sets:
                used[s] += begins
        self.used = used
        self.used0 = [a + before.times * b for a, b in zip(before.used0, before.used)] if before else [0] * 4
        self.slabs = 2 * len(body)

    def block(self, i, b):
        return i * len(self.body) + (self.block0 + b)

    def raw_slot(self, b):
        return (self.block0 + b) % 2

    def raw_count(self, i, b):
        return i * (8 * len(self.body)) + 16 * ((self.block0 + b) // 2 + 1)

    def slab(self, i, k):
        return i * self.slabs + (2 * self.block0 + k)

    def slot(self, k):
        return (2 * self.block0 + k) % 4

    def set_uses(self, i, k):
        s = self.body[k // 2][2][k % 2]
        begun = sum(blk[3] for blk in self.body[:k // 2 + 1] if s in blk[2])
        return i * self.used[s] + (self.used0[s] + begun - 1)


PAIR_BODY = [(0, DC, (0, 1), True, True), (0, DC, (2, 3), True, True)]
DOWN_BODY = [(sum(DOWN_K[:r]), DOWN_K[r], sets, r == 0, r == 3) for sets in ((0, 1), (2, 3)) for r in range(4)]


def wait_from_one(eng, sem, value):
    if not isinstance(value, int) or value > 0:
        eng.wait_ge(sem, value)


def layer(nc, x_in, gu_a, down_a, w_in, w_out, gu_b, down_b, consts, vecs, lams, lora, g2,
          cache_k, cache_v, pages, state_in, shift_in,
          y_out, k_out, v_out, wkv_out, shift_out, wkv_s_out):
    f32, f32r, i32 = mybir.dt.float32, mybir.dt.float32r, mybir.dt.int32
    ALU, ACT, AX = mybir.AluOpType, mybir.ActivationFunctionType, mybir.AxisListType

    up_a = Product(PAIR_BODY, FC // 2)
    dn_a = Product(DOWN_BODY, 2, up_a)
    inp = Product(PAIR_BODY, 6, dn_a)
    inp_tail = Product(PAIR_BODY[:1], 1, inp)
    outp = Product(PAIR_BODY, 2, inp_tail)
    up_b = Product(PAIR_BODY, FC // 2, outp)
    dn_b = Product(DOWN_BODY, 2, up_b)

    hi_dram = nc.dram_tensor("trunk_hi", (P, DC, TOK), f32, kind="Internal").ap()
    lo_dram = nc.dram_tensor("trunk_lo", (P, DC, TOK), f32, kind="Internal").ap()

    ctx = ExitStack()
    with ctx:
        def sb(name, shape, dt=f32, to=ctx):
            return to.enter_context(nc.sbuf_tensor(name, shape, dt))

        def sem(name):
            return ctx.enter_context(nc.semaphore(name))

        acc = [ctx.enter_context(nc.psum_tensor(f"acc{n}", [P, 2, 512], f32)) for n in range(4)]

        trunk = ExitStack()
        XH = sb("x_hi", [P, DC, TOK], f32r, trunk)
        XL = sb("x_lo", [P, DC, TOK], f32r, trunk)
        RAW = [sb(f"weights_raw{n}", [P, DC, 2 * P], f32, trunk) for n in range(2)]
        WH = [sb(f"weights_hi{n}", [P, DC, P], f32r, trunk) for n in range(4)]
        WL = [sb(f"weights_lo{n}", [P, DC, P], f32r, trunk) for n in range(4)]
        trunk.close()
        mixing = ExitStack()
        U = sb("head_tiles", [P, 11, TOK], f32, mixing)
        BD = [sb(f"blocks_{n}", [P, NCH, P], f32, mixing) for n in "abkrv"]
        TT, MT, RBT, RKT, PP, PT, YY, EE = (
            sb(n, [P, NCH, P], f32, mixing)
            for n in ("t_turned", "m_turned", "rb_turned", "rk_turned", "inverse", "inverse_turned", "level_y", "level_e"))
        TK = {n: sb(f"tokens_{c}", [P, NCH, P], f32, mixing) for n, c in ((1, "b"), (2, "k"), (4, "v"))}
        LAST = sb("last_state", [P, P], f32, mixing)
        mixing.close()
        region = sb("first_region", [P, 4 * (11 * TOK + (5 + 8 + 3) * NCH * P + P)], mybir.dt.uint8)

        Y = sb("y_sum", [P, DC, TOK])
        SCR = sb("scratch", [P, 6, TOK])
        VEC = sb("feature_vectors", [P, NVEC])
        MEAN = sb("mean_weights", [P, P])
        EPS = sb("epsilons", [P, 5])
        COS, SIN = Y[:, 6, :], Y[:, 7, :]

        ffn = ExitStack()
        HH = sb("hidden_hi", [P, FC, TOK], f32r, ffn)
        HL = sb("hidden_lo", [P, FC, TOK], f32r, ffn)
        ffn.close()
        mixed = ExitStack()
        MH = sb("mixed_hi", [P, DC, TOK], f32r, mixed)
        ML = sb("mixed_lo", [P, DC, TOK], f32r, mixed)
        mixed.close()
        PROJ = sb("projected", [P, IN_CHUNKS, TOK])
        CONST = sb("constants", [P, NCONST])
        KP = sb("key_pages", [P, KS, 512])
        VP = sb("value_pages", [P, VS, 512])
        QB = sb("query_rows", [P, 512])
        XWA = sb("decay_rate_inputs", [P, TOK])
        XSG = sb("gate_inputs", [P, TOK])
        LORA, LG2 = sb("lora_w2_a2", [P, P]), sb("lora_g2", [P, P])
        LAMV, LAM = sb("lambda_vectors", [P, 256]), sb("lambda", [P, 8])
        SHIFT = sb("shift_rows", [P, RC, DEC])
        QK, OWN = sb("own_key_products", [P, 4, DEC]), sb("own_logits", [P, DEC, 4, 2])
        ID2 = sb("stacked_identity", [P, 64])
        TABLE = sb("page_ids", [1, DEC * PAGES], i32)
        L, SM = sb("decode_logits", [P, PAGES + 1, 8]), sb("decode_small", [P, 32])
        AD = sb("decode_weights", [P, PAGES + 1, 4])
        SMP = sb("prompt_small", [P, 8])
        PV, PVS, GAIN = sb("pair_vectors", [P, 10]), sb("pair_vectors_s", [P, 10]), sb("gains", [P, NCH])

        sems = {}

        def g(name):
            if name not in sems:
                sems[name] = sem(name)
            return sems[name]

        raw_ready = [sem(f"raw_ready{n}") for n in range(2)]
        split_hi, split_lo, slab_used = sem("split_hi"), sem("split_lo"), sem("slab_used")
        acc_free = [sem(f"acc_free{n}") for n in range(4)]
        tables_in, consts_set = sem("tables_in"), sem("consts_set")
        x_loaded = [sem(f"x_loaded{n}") for n in range(DC // 2)]
        x_hi, x_ready = sem("x_hi_done"), sem("x_ready")
        gated, hidden, h_hi, h_ready = sem("gated"), sem("hidden"), sem("h_hi"), sem("h_ready")
        y_ready, y_part = sem("y_ready"), sem("y_part")
        mean_done, centered, squared, var_done, std_done, rstd_done, scaled = (
            sem(n) for n in ("mean_done", "centered", "squared", "var_done", "std_done", "rstd_done", "scaled"))
        stored = sem("stored")
        proj_ready = sem("proj_ready")

        def halves(t):
            return t.rearrange("p (a n) -> p a n", a=2)

        def accv(s):
            return acc[s][:, :, 0:HALF]

        def load_weights(sp, pr, i, src):
            for b, (k0, nk, _, _, _) in enumerate(pr.body):
                wait_from_one(sp, split_lo, 2 * (pr.block(i, b) - 1))
                slot = pr.raw_slot(b)
                sp.dma_start(RAW[slot][:, 0:nk, :], src(i, b)).then_inc(raw_ready[slot], 16)

        def split_high(act, pr, i, k):
            b = k // 2
            nk, slot = pr.body[b][1], pr.raw_slot(b)
            act.wait_ge(raw_ready[slot], pr.raw_count(i, b))
            wait_from_one(act, slab_used, pr.slab(i, k) - 3)
            nc.scalar.activation(WH[pr.slot(k)][:, 0:nk, :], RAW[slot][:, 0:nk, P * (k % 2):P * (k % 2) + P],
                                 ACT.Copy).then_inc(split_hi, 1)

        def split_low(dve, pr, i, k):
            b = k // 2
            nk, slot = pr.body[b][1], pr.raw_slot(b)
            dve.wait_ge(split_hi, pr.slab(i, k) + 1)
            nc.vector.tensor_tensor(WL[pr.slot(k)][:, 0:nk, :], RAW[slot][:, 0:nk, P * (k % 2):P * (k % 2) + P],
                                    WH[pr.slot(k)][:, 0:nk, :].bitcast(f32), ALU.subtract).then_inc(split_lo, 1)

        def multiply(pe, pr, i, hi, lo, ready=None, order=None):
            for k in range(pr.slabs):
                k0, nk, sets, begins, ends = pr.body[k // 2]
                s, slot = sets[k % 2], pr.slot(k)
                pe.wait_ge(split_lo, pr.slab(i, k) + 1)
                if begins:
                    wait_from_one(pe, acc_free[s], pr.set_uses(i, k))
                tiles = order if order and k == 0 else list(range(nk))
                for t in tiles:
                    if ready and k == 0:
                        pe.wait_ge(ready[0], ready[1] + tiles.index(t) + 1)
                    for n, (w, x) in enumerate(((WH, hi), (WH, lo), (WL, hi))):
                        for a in range(2):
                            mm = nc.tensor.matmul(acc[s][:, a, 0:HALF], w[slot][:, t, :],
                                                  x[:, k0 + t, HALF * a:HALF * a + HALF],
                                                  start=begins and t == tiles[0] and n == 0,
                                                  stop=ends and t == tiles[-1] and n == 2)
                mm.then_inc(slab_used, 1)

        def gate_up_scalar(act, pr, u, i, split, drain):
            for k in range(4):
                if split:
                    split_high(act, pr, i, k)
                if drain and k < 2:
                    act.wait_ge(slab_used, pr.slab(i - 1, k) + 1)
                    wait_from_one(act, hidden, 2 * (i - 2) + k + 1 + u * FC)
                    nc.scalar.activation(halves(SCR[:, k, :]), accv(k), ACT.Silu).then_inc(acc_free[k], 1)
                if drain and k >= 2:
                    act.wait_ge(hidden, 2 * (i - 1) + k - 1 + u * FC)
                    nc.scalar.activation(HH[:, bass.ds(2 * (i - 1) + k - 2, 1), :], SCR[:, k:k + 1, :],
                                         ACT.Copy).then_inc(h_hi, 1)

        def gate_up_vector(dve, pr, u, i, split, drain):
            for k in range(4):
                if split:
                    split_low(dve, pr, i, k)
                if drain and k >= 2:
                    c = 2 * (i - 1) + k - 2
                    dve.wait_ge(acc_free[k - 2], pr.set_uses(i - 1, k - 2) + 1)
                    dve.wait_ge(slab_used, pr.slab(i - 1, k) + 1)
                    dve.tensor_tensor(halves(SCR[:, k, :]), halves(SCR[:, k - 2, :]), accv(k),
                                      ALU.mult).then_inc(hidden, 1)
                    dve.wait_ge(h_hi, c + 1 + u * FC)
                    dve.tensor_tensor(HL[:, bass.ds(c, 1), :], SCR[:, k:k + 1, :],
                                      HH[:, bass.ds(c, 1), :].bitcast(f32), ALU.subtract).then_inc(acc_free[k], 1)

        def residual(dve, pr, i, k, c, coef):
            s = pr.body[k // 2][2][k % 2]
            dve.wait_ge(slab_used, pr.slab(i, k) + 1)
            chunk = halves(Y[:, bass.ds(c, 1), :].rearrange("p a n -> p (a n)"))
            xh = halves(XH[:, bass.ds(c, 1), :].rearrange("p a n -> p (a n)").bitcast(f32))
            xl = halves(XL[:, bass.ds(c, 1), :].rearrange("p a n -> p (a n)").bitcast(f32))
            nc.vector.scalar_tensor_tensor(out=chunk, in0=xh, scalar=coef, in1=accv(s), op0=ALU.mult,
                                           op1=ALU.add).then_inc(acc_free[s], 1)
            dve.wait_ge(acc_free[s], pr.set_uses(i, k) + 1)
            nc.vector.scalar_tensor_tensor(out=chunk, in0=xl, scalar=coef, in1=chunk, op0=ALU.mult,
                                           op1=ALU.add).then_inc(y_ready, 1)

        def down_tensor(pe, pr, u):
            for s in (2, 3):
                pe.wait_ge(acc_free[s], pr.used0[s])
            with pe.Fori(0, pr.times) as i:
                multiply(pe, pr, i, HH, HL)

        def down_scalar(act, pr):
            with act.Fori(0, pr.times) as i:
                for k in range(pr.slabs):
                    split_high(act, pr, i, k)

        def down_vector(dve, pr):
            with dve.Fori(0, pr.times) as i:
                for k in range(pr.slabs):
                    split_low(dve, pr, i, k)
                    for e, c in ((6, 0), (7, 1), (14, 2), (15, 3)):
                        if k == min(e + 4, pr.slabs - 1):
                            residual(dve, pr, i, e, i * 4 + c, 2 * ALPHA)

        def norm_tensor(pe, n):
            pe.wait_ge(y_ready, DC * n + 6)
            pe.wait_ge(g("chunks_summed"), (DC - 2) * (n + 1))
            for a in range(2):
                nc.tensor.matmul(acc[0][:, a, 0:HALF], MEAN[:, :], SCR[:, 5, HALF * a:HALF * a + HALF],
                                 start=True, stop=False)
            pe.wait_ge(y_ready, DC * n + DC)
            for a in range(2):
                mm = nc.tensor.matmul(acc[0][:, a, 0:HALF], MEAN[:, :], Y[:, DC - 1, HALF * a:HALF * a + HALF],
                                      start=False, stop=True)
            mm.then_inc(mean_done, 1)
            for c in range(DC):
                pe.wait_ge(squared, DC * n + c + 1)
                for a in range(2):
                    mm = nc.tensor.matmul(acc[1][:, a, 0:HALF], MEAN[:, :],
                                          SCR[:, 2 + c % 2, HALF * a:HALF * a + HALF],
                                          start=c == 0, stop=c == DC - 1)
                mm.then_inc(var_done, 1)

        def norm_pool(pool, n):
            if n:
                pool.wait_ge(mean_done, n)
            for c in range(1, DC - 1):
                pool.wait_ge(y_ready, DC * n + c + 1)
                if c > 1:
                    pool.wait_ge(g("chunks_summed"), (DC - 2) * n + c - 1)
                pool.tensor_tensor(SCR[:, 5, :], Y[:, 0, :] if c == 1 else SCR[:, 5, :], Y[:, c, :], ALU.add)\
                    .then_inc(g("chunks_summed"), 1)

        def norm_scalar(act, n, following=None, out=None):
            if following:
                for k in range(4):
                    split_high(act, following, 0, k)
            for c in range(DC):
                act.wait_ge(centered, DC * n + c + 1)
                if DC * n + c >= 2:
                    act.wait_ge(var_done, DC * n + c - 1)
                nc.scalar.activation(SCR[:, 2 + c % 2, :], Y[:, c, :], ACT.Square).then_inc(squared, 1)
            act.wait_ge(var_done, DC * n + DC)
            nc.scalar.activation(halves(SCR[:, 4, :]), accv(1), ACT.Sqrt, bias=EPS[:, n:n + 1]).then_inc(std_done, 1)
            for c in range(DC):
                act.wait_ge(scaled, DC * n + c + 1)
                bias = VEC[:, V_LN + (2 * n + 1) * DC + c:V_LN + (2 * n + 1) * DC + c + 1]
                if out is None:
                    nc.scalar.activation(XH[:, c, :], Y[:, c, :], ACT.Identity, bias=bias).then_inc(x_hi, 1)
                else:
                    nc.scalar.activation(Y[:, c, :], Y[:, c, :], ACT.Identity, bias=bias).then_inc(x_hi, 1)

        def norm_vector(dve, n, following=None, last=False):
            if following:
                for k in range(4):
                    split_low(dve, following, 0, k)
            dve.wait_ge(mean_done, n + 1)
            for c in range(DC):
                nc.vector.tensor_tensor(halves(Y[:, c, :]), halves(Y[:, c, :]), accv(0),
                                        ALU.subtract).then_inc(centered, 1)
            dve.wait_ge(std_done, n + 1)
            nc.vector.reciprocal(SCR[:, 5, :], SCR[:, 4, :]).then_inc(rstd_done, 1)
            dve.wait_ge(rstd_done, n + 1)
            for c in range(DC):
                g = V_LN + 2 * n * DC + c
                nc.vector.scalar_tensor_tensor(out=Y[:, c, :], in0=Y[:, c, :], scalar=VEC[:, g:g + 1],
                                               in1=SCR[:, 5, :], op0=ALU.mult, op1=ALU.mult).then_inc(scaled, 1)
                if not last and c >= 1:
                    low_part(dve, n, c - 1)
            if not last:
                low_part(dve, n, DC - 1)

        def low_part(dve, n, c):
            b = V_LN + (2 * n + 1) * DC + c
            dve.wait_ge(x_hi, DC * (n + 1) + c + 1)
            nc.vector.scalar_tensor_tensor(out=XL[:, c, :], in0=Y[:, c, :], scalar=VEC[:, b:b + 1],
                                           in1=XH[:, c, :].bitcast(f32), op0=ALU.add,
                                           op1=ALU.subtract).then_inc(x_ready, 1)

        def to_projected(act, pr, i, k, c):
            act.wait_ge(slab_used, pr.slab(i, k) + 1)
            nc.scalar.activation(halves(PROJ[:, bass.ds(c, 1), :].rearrange("p a n -> p (a n)")),
                                 accv(pr.body[k // 2][2][k % 2]), ACT.Copy)\
                .then_inc(acc_free[pr.body[k // 2][2][k % 2]], 1)

        def input_scalar(act):
            def step(i, split, drain):
                for k in range(4):
                    if split:
                        split_high(act, inp, i, k)
                    if drain:
                        to_projected(act, inp, i - 1, k, (i - 1) * 4 + k)
            with act.Fori(1, inp.times) as i:
                step(i, True, True)
            for k in range(4):
                if k < 2:
                    split_high(act, inp_tail, 0, k)
                to_projected(act, inp, inp.times - 1, k, 4 * (inp.times - 1) + k)
            for k in range(2):
                to_projected(act, inp_tail, 0, k, 4 * inp.times + k)

        def gate_up(step, eng, pr, u):
            step(eng, pr, u, 1, True, True)
            with eng.Fori(2, pr.times) as i:
                step(eng, pr, u, i, True, True)
            step(eng, pr, u, pr.times, False, True)

        def gate_up_tensor(pe, pr, n):
            multiply(pe, pr, 0, XH, XL, (x_ready, DC * n))
            with pe.Fori(1, pr.times) as i:
                multiply(pe, pr, i, XH, XL)

        def pj(c):
            return PROJ[:, bass.ds(c, 1), :].rearrange("p a n -> p (a n)")

        def projected(eng):
            for s in range(4):
                eng.wait_ge(acc_free[s], outp.used0[s])

        def const(c, n=P):
            return CONST[:, c:c + n]

        def bank(n):
            return acc[n // 2][:, n % 2, :]

        def shift(dve, chain, out, c, last, mu):
            tmp, cur = SCR[:, 5, :], pj(c)
            nc.vector.tensor_tensor(tmp[:, 1:SEQ], cur[:, 0:SEQ - 1], cur[:, 1:SEQ], ALU.subtract)
            nc.vector.tensor_scalar(tmp[:, 0:1], cur[:, 0:1], -1.0, None, ALU.mult)
            chain(nc.vector.tensor_tensor(tmp[:, SEQ:TOK], last, cur[:, SEQ:TOK], ALU.subtract))
            return nc.vector.scalar_tensor_tensor(out=out, in0=tmp, scalar=mu, in1=cur, op0=ALU.mult, op1=ALU.add)

        class Chain:

            def __init__(self, eng, sem, turn=0, per_turn=0, before=0):
                self.eng, self.sem, self.turn, self.per_turn, self.n, self.before = eng, sem, turn, per_turn, 0, before

            def __call__(self, ins):
                self.n += 1
                ins.then_inc(self.sem, 1)
                self.eng.wait_ge(self.sem, self.turn * self.per_turn + (self.before + self.n))

            def end(self):
                assert self.n == self.per_turn, (self.sem.name, self.n)

        def prelude_tensor(pe):
            projected(pe)
            pe.wait_ge(g("consts_in"), 16)
            for c in range(2 * DA_HEADS):
                if c >= 4:
                    pe.wait_ge(g("rope_sin"), c - 3)
                for a in range(2):
                    mm = nc.tensor.matmul(acc[c % 4][:, a, 0:HALF], const(C_SWAP), PROJ[:, c, HALF * a:HALF * a + HALF],
                                          start=True, stop=True)
                mm.then_inc(g("rope_swapped"), 1)
            pe.wait_ge(g("own_products"), 1)
            for m in range(2):
                mm = nc.tensor.matmul(bank(m)[:, 0:32], MEAN[64 * m:64 * m + 64, :], QK[64 * m:64 * m + 64, :, :],
                                      start=True, stop=True)
            mm.then_inc(g("own_summed"), 1)

        def prelude_pool(pool):
            projected(pool)
            pool.wait_ge(g("consts_in"), 16)
            for c in range(2 * DA_HEADS):
                if c >= 2:
                    pool.wait_ge(g("roped"), c - 1)
                pool.tensor_tensor(SCR[:, 2 + c % 2, :], PROJ[:, c, :], COS, ALU.mult).then_inc(g("rope_cos"), 1)

        def prelude_vector(dve):
            projected(dve)
            dve.wait_ge(g("consts_in"), 16)
            dve.wait_ge(g("small_in"), 48)
            chain = Chain(dve, g("dve_prelude"))
            nc.vector.tensor_tensor(LAMV[:, 0:64], LAMV[:, 0:64], LAMV[:, 64:128], ALU.mult)
            chain(nc.vector.tensor_tensor(LAMV[:, 128:192], LAMV[:, 128:192], LAMV[:, 192:256], ALU.mult))
            nc.vector.reduce_sum(LAM[:, 0:1], LAMV[:, 0:64], AX.X)
            nc.vector.reduce_sum(LAM[:, 1:2], LAMV[:, 128:192], AX.X).then_inc(g("lam_sums"), 1)
            nc.vector.tensor_tensor(ID2[:, :], const(C_ID, 64), const(C_ID + 64, 64), ALU.add)
            for c in range(2 * DA_HEADS):
                dve.wait_ge(g("rope_swapped"), c + 1)
                nc.vector.tensor_tensor(halves(SCR[:, c % 2, :]), accv(c % 4), halves(SIN),
                                        ALU.mult).then_inc(g("rope_sin"), 1)
                dve.wait_ge(g("rope_sin"), c + 1)
                dve.wait_ge(g("rope_cos"), c + 1)
                nc.vector.tensor_tensor(PROJ[:, c, :], SCR[:, c % 2, :], SCR[:, 2 + c % 2, :], ALU.add)\
                    .then_inc(g("roped"), 1)
            dve.wait_ge(g("lam_exps"), 1)
            chain(nc.vector.tensor_tensor(LAM[:, 0:1], LAM[:, 3:4], LAM[:, 2:3], ALU.subtract))
            chain(nc.vector.tensor_scalar(LAM[:, 4:5], LAM[:, 0:1], -LAM_INIT, None, ALU.add))
            chain(shift(dve, chain, XWA[:, :], 24, SHIFT[:, 12, :], VEC[:, V_MU2:V_MU2 + 1]))
            shift(dve, chain, XSG[:, :], 25, SHIFT[:, 13, :], VEC[:, V_MU2 + 1:V_MU2 + 2]).then_inc(g("lora_in"), 1)
            dve.wait_ge(g("roped"), 8)
            nc.vector.tensor_tensor(QK[:, :, :], PROJ[:, 0:4, SEQ:TOK], PROJ[:, 4:8, SEQ:TOK],
                                    ALU.mult).then_inc(g("own_products"), 1)
            nc.vector.memset(SM[:, :], 0.0).then_inc(g("d_out"), 1)
            dve.wait_ge(g("own_summed"), 1)
            for m in range(2):
                ins = nc.vector.tensor_scalar(OWN[:, :, :, m].rearrange("p b h -> p h b"),
                                              bank(m)[:, 0:32].rearrange("p (h b) -> p h b", b=DEC),
                                              float(D_MODEL), None, ALU.mult)
            ins.then_inc(g("own_ready"), 1)

        def prelude_scalar(act):
            act.wait_ge(g("lam_sums"), 1)
            nc.scalar.activation(LAM[:, 2:4], LAM[:, 0:2], ACT.Exp).then_inc(g("lam_exps"), 1)
            act.wait_ge(g("lora_in"), 1)
            nc.scalar.activation(XWA[0:64, :], XWA[0:64, :], ACT.Tanh)
            nc.scalar.activation(XSG[:, :], XSG[:, :], ACT.Sigmoid).then_inc(g("lora_act"), 1)

        def decode_loads(sp):
            def page(b, n, cache, dst, done, freed, slots):
                pid = sp.value_load(TABLE[0:1, bass.ds(b * PAGES + n, 1)], min_val=0, max_val=POOL - 1)
                wait_from_one(sp, freed, b * PAGES + (n - slots + 1))
                sp.dma_start(dst, cache[bass.ds(pid, 1), :, :].rearrange("a p n -> (a p) n")).then_inc(done, 16)

            def k_page(b, n):
                page(b, n, cache_k, KP[:, n % KS, :], g(f"k_in{n % KS}"), g("k_reduced"), KS)

            def v_page(b, n):
                page(b, n, cache_v, VP[:, n % VS, :], g(f"v_in{n % VS}"), g("v_used"), VS)

            def turn(i, more):
                b = 2 * i
                for n in range(KS, PAGES):
                    k_page(b, n)
                for n in range(VS):
                    v_page(b, n)
                for n in range(KS):
                    k_page(b + 1, n)
                for n in range(VS, PAGES, VS):
                    for m in range(n, n + VS):
                        v_page(b, m)
                    for m in range(n, n + KS):
                        k_page(b + 1, m)
                for n in range(VS):
                    v_page(b + 1, n)
                if more:
                    for n in range(KS):
                        k_page(b + 2, n)
                for n in range(VS, PAGES):
                    v_page(b + 1, n)

            for n in range(KS):
                k_page(0, n)
            turn(0, True)
            with sp.Fori(1, DA_HEADS - 1) as i:
                turn(i, True)
            turn(DA_HEADS - 1, False)

        def decode_query_pool(pool, b):
            pool.tensor_copy(QB[:, :].rearrange("p (h n) -> p h n", n=P), PROJ[:, 0:4, bass.ds(b + SEQ, 1)].broadcast_to([P, 4, P]))\
                .then_inc(g("q_column"), 1)

        def decode_query_tensor(pe, b, bk, second):
            pe.wait_ge(g("q_column"), b + 1)
            if second:
                pe.wait_ge(g("weights_d"), b)
            else:
                pe.wait_ge(g("d_out"), b + 1)
            for h in range(DA_HEADS):
                mm = nc.tensor.matmul(bank(bk)[:, P * h:P * h + P], QB[:, P * h:P * h + P], const(C_ID), start=True, stop=True)
            mm.then_inc(g("q_spread"), 1)

        def decode_query_scalar(act, b, bk):
            act.wait_ge(g("q_spread"), b + 1)
            nc.scalar.activation(QB[:, :], bank(bk), ACT.Copy).then_inc(g("q_rows"), 1)

        def decode_pages_pool(pool, b, pages):
            pool.wait_ge(g("q_rows"), b + 1)
            for n in pages:
                pool.wait_ge(g(f"k_in{n % KS}"), b * (16 * PAGES // KS) + 16 * (n // KS + 1))
                pool.tensor_tensor(KP[:, n % KS, :], KP[:, n % KS, :], QB[:, :], ALU.mult).then_inc(g("k_multiplied"), 1)
                if n == PAGES - 1:
                    pool.wait_ge(g("k_multiplied"), b * PAGES + PAGES)

        def decode_pages_vector(dve, b, pages):
            for n in pages:
                dve.wait_ge(g("k_multiplied"), b * PAGES + (n + 1))
                nc.vector.reduce_sum(L[:, n, :], KP[:, n % KS, :].rearrange("p (g d) -> p g d", d=DA_QK),
                                     AX.X).then_inc(g("k_reduced"), 1)

        def decode_softmax_vector(dve, b, bk, chain, part):
            if part == 0:
                chain(nc.vector.tensor_copy(L[:, PAGES, :], OWN[:, bass.ds(b, 1), :, :].rearrange("p b h m -> p (b h m)")))
                nc.vector.reduce_max(SM[:, 0:8], L[:, :, :].rearrange("p n g -> p g n"), AX.X).then_inc(g("max_part"), 1)
            if part == 1:
                dve.wait_ge(g("max_turned"), b + 1)
                chain(nc.vector.reduce_max(SM[0:8, 8:9], bank(bk)[0:8, 0:P], AX.X))
                nc.vector.tensor_scalar(SM[0:8, 16:24], CONST[0:8, C_ID:C_ID + 8], SM[0:8, 8:9], None,
                                        ALU.mult).then_inc(g("max_diag"), 1)
            if part == 2:
                dve.wait_ge(g("max_spread"), b + 1)
                chain(nc.vector.tensor_scalar(SM[:, 8:16], bank(bk)[:, P:P + 8], float(D_MODEL), None, ALU.mult))
                nc.vector.tensor_tensor(L[:, :, :], L[:, :, :], SM[:, 8:16].unsqueeze(1).broadcast_to([P, PAGES + 1, 8]),
                                        ALU.subtract).then_inc(g("l_centered"), 1)
            if part == 3:
                dve.wait_ge(g("l_exp"), b + 1)
                nc.vector.reduce_sum(SM[:, 24:32], L[:, 0:PAGES, :].rearrange("p n g -> p g n"), AX.X)\
                    .then_inc(g("sum_part"), 1)
            if part == 4:
                dve.wait_ge(g("sum_spread"), b + 1)
                chain(nc.vector.scalar_tensor_tensor(out=SM[:, 0:8], in0=bank(bk)[:, P + 8:P + 16], scalar=float(D_MODEL),
                                                     in1=L[:, PAGES, :], op0=ALU.mult, op1=ALU.add))
                chain(nc.vector.reciprocal(SM[:, 8:16], SM[:, 0:8]))
                chain(nc.vector.tensor_scalar(SM[:, 9:16:2], SM[:, 9:16:2], LAM[:, 4:5], None, ALU.mult))
                chain(nc.vector.tensor_tensor(L[:, :, :], L[:, :, :],
                                              SM[:, 8:16].unsqueeze(1).broadcast_to([P, PAGES + 1, 8]), ALU.mult))
                nc.vector.tensor_tensor(AD[:, :, :], L[:, :, 0:8:2], L[:, :, 1:8:2], ALU.add).then_inc(g("weights_d"), 1)

        def decode_softmax_scalar(act, b):
            act.wait_ge(g("l_centered"), b + 1)
            nc.scalar.activation(L[:, :, :], L[:, :, :], ACT.Exp, scale=SCALE).then_inc(g("l_exp"), 1)

        def decode_softmax_tensor(pe, b, bk, part):
            if part == 0:
                pe.wait_ge(g("max_part"), b + 1)
                nc.tensor.transpose(bank(bk)[0:8, 0:P], SM[:, 0:8], const(C_ID)).then_inc(g("max_turned"), 1)
            if part == 1:
                pe.wait_ge(g("max_diag"), b + 1)
                nc.tensor.matmul(bank(bk)[:, P:P + 8], MEAN[0:8, :], SM[0:8, 16:24], start=True, stop=True)\
                    .then_inc(g("max_spread"), 1)
            if part == 3:
                pe.wait_ge(g("sum_part"), b + 1)
                nc.tensor.matmul(bank(bk)[:, P + 8:P + 16], MEAN[:, :], SM[:, 24:32], start=True, stop=True)\
                    .then_inc(g("sum_spread"), 1)

        def decode_values_tensor(pe, b, bk, pages):
            pe.wait_ge(g("weights_d"), b + 1)
            for n in pages:
                pe.wait_ge(g(f"v_in{n % VS}"), b * (16 * PAGES // VS) + 16 * (n // VS + 1))
                for h in range(DA_HEADS):
                    mm = nc.tensor.matmul(bank(bk)[:, h:h + 1], VP[:, n % VS, P * h:P * h + P], AD[:, n, h:h + 1],
                                          start=n == 0 and h == 0, stop=n == PAGES - 1, skip_group_check=True)
                mm.then_inc(g("v_used"), 1)

        def decode_values_vector(dve, b, bk, chain):
            chain(nc.vector.tensor_tensor(SM[:, 0:4].unsqueeze(2), PROJ[:, 8:12, bass.ds(b + SEQ, 1)],
                                          AD[:, PAGES, :].unsqueeze(2), ALU.mult))
            dve.wait_ge(g("v_used"), b * PAGES + PAGES)
            nc.vector.tensor_tensor(Y[:, 0:4, bass.ds(b + SEQ, 1)], SM[:, 0:4].unsqueeze(2),
                                    bank(bk)[:, 0:4].unsqueeze(2), ALU.add).then_inc(g("d_out"), 1)

        QS, KSB, VSB, VT = (U[:, n, 0:SEQ] for n in (0, 1, 2, 3))
        PR = (U[:, 4, 0:SEQ], U[:, 6, 0:SEQ])
        AW = U[:, 7, 0:SEQ]
        AT = SCR[:, 1:5, 0:SEQ]
        QT_TILES = SEQ // P
        ATT_BANK = 6

        def attention_begin_scalar(act, i):
            act.wait_ge(g("bd_ready"), i + 1)
            act.wait_ge(g("r_blocks"), i * 2 + 2)
            act.wait_ge(g("rk_summed"), i + 1)
            nc.scalar.activation(QS, pj(i)[:, 0:SEQ], ACT.Copy)
            nc.scalar.activation(KSB, pj(i + 4)[:, 0:SEQ], ACT.Copy)
            act.wait_ge(g("bonus"), i + 1)
            nc.scalar.activation(VSB, pj(i + 8)[:, 0:SEQ], ACT.Copy).then_inc(g("head_copied"), 1)

        def attention_v_scalar(act, i):
            act.wait_ge(g("v_turned"), i + 1)
            nc.scalar.activation(VT, bank(ATT_BANK), ACT.Copy).then_inc(g("vt_copied"), 1)

        def attention_v_tensor(pe, i):
            pe.wait_ge(g("head_copied"), i + 1)
            for t in range(QT_TILES):
                mm = nc.tensor.transpose(bank(ATT_BANK)[:, P * t:P * t + P], VSB[:, P * t:P * t + P], const(C_ID))
            mm.then_inc(g("v_turned"), 1)

        def attention_logits_tensor(pe, i, qt):
            for m in range(2):
                if qt >= 1:
                    pe.wait_ge(g("exped"), i * 8 + (2 * (qt - 1) + m + 1))
                out = bank(4 + m)
                rows = slice(64 * m, 64 * m + 64)
                nc.tensor.matmul(out[:, 0:P * (qt + 1)], QS[rows, P * qt:P * qt + P], KSB[rows, 0:P * (qt + 1)],
                                 start=True, stop=False)
                nc.tensor.matmul(out[:, P * qt:P * qt + P], const(C_ID), const(C_CAUSAL), start=False,
                                 stop=True).then_inc(g("logits"), 1)

        def attention_turn_tensor(pe, i, qt):
            pe.wait_ge(g("weights_p"), i * 4 + (qt + 1))
            if qt:
                pe.wait_ge(g("at_copied"), i * 4 + qt)
            else:
                pe.wait_ge(g("vt_copied"), i + 1)
            for kb in range(qt + 1):
                mm = nc.tensor.transpose(bank(ATT_BANK)[:, P * kb:P * kb + P], AW[:, P * kb:P * kb + P], const(C_ID))
            mm.then_inc(g("aw_turned"), 1)

        def attention_values_tensor(pe, i):
            pe.wait_ge(g("at_copied"), i * 4 + 4)
            for kb in range(QT_TILES):
                mm = nc.tensor.matmul(bank(ATT_BANK)[:, P * kb:SEQ], VT[:, P * kb:P * kb + P], AT[:, kb, P * kb:SEQ],
                                      start=kb == 0, stop=kb == QT_TILES - 1)
            mm.then_inc(g("pv_done"), 1)

        def attention_exp_scalar(act, i, qt):
            for m in range(2):
                act.wait_ge(g("max_neg"), i * 8 + (2 * qt + m + 1))
                if qt >= 1:
                    act.wait_ge(g("weights_p"), i * 4 + qt)
                nc.scalar.activation(PR[m][:, 0:P * (qt + 1)], bank(4 + m)[:, 0:P * (qt + 1)], ACT.Exp,
                                     bias=SMP[:, 2 + m:3 + m], scale=SCALE,
                                     accum_out=SMP[:, 4 + m:5 + m]).then_inc(g("exped"), 1)

        def attention_turn_scalar(act, i, qt):
            act.wait_ge(g("aw_turned"), i * 4 + (qt + 1))
            nc.scalar.activation(AT[:, 0:qt + 1, P * qt:P * qt + P],
                                 bank(ATT_BANK)[:, 0:P * (qt + 1)].rearrange("p (k q) -> p k q", q=P),
                                 ACT.Copy).then_inc(g("at_copied"), 1)

        def attention_out_scalar(act, i):
            act.wait_ge(g("pv_done"), i + 1)
            nc.scalar.activation(Y[:, bass.ds(i, 1), 0:SEQ].rearrange("p a n -> p (a n)"), bank(ATT_BANK), ACT.Copy)\
                .then_inc(g("head_out"), 1)

        def attention_max_vector(dve, i, qt, chain):
            for m in range(2):
                dve.wait_ge(g("logits"), i * 8 + (2 * qt + m + 1))
                chain(nc.vector.reduce_max(SMP[:, m:m + 1], bank(4 + m)[:, 0:P * (qt + 1)], AX.X))
                nc.vector.tensor_scalar(SMP[:, 2 + m:3 + m], SMP[:, m:m + 1], -SCALE, None,
                                        ALU.mult).then_inc(g("max_neg"), 1)

        def attention_weights_vector(dve, i, qt, chain):
            dve.wait_ge(g("exped"), i * 8 + (2 * qt + 2))
            chain(nc.vector.reciprocal(SMP[:, 6:8], SMP[:, 4:6]))
            chain(nc.vector.tensor_scalar(SMP[:, 7:8], SMP[:, 7:8], LAM[:, 4:5], None, ALU.mult))
            w = P * (qt + 1)
            if qt >= 1:
                dve.wait_ge(g("aw_turned"), i * 4 + qt)
            chain(nc.vector.tensor_scalar(AW[:, 0:w], PR[0][:, 0:w], SMP[:, 6:7], None, ALU.mult))
            nc.vector.scalar_tensor_tensor(out=AW[:, 0:w], in0=PR[1][:, 0:w], scalar=SMP[:, 7:8], in1=AW[:, 0:w],
                                           op0=ALU.mult, op1=ALU.add).then_inc(g("weights_p"), 1)

        XR, XK, XV, LW, AG, GG, KK, K2, BB, BO, T1 = (U[:, n, :] for n in range(11))
        CUM, DD, E1, E2, E3, OT = (SCR[:, n, :] for n in (0, 1, 2, 3, 4, 0))
        A_, B_, K_, R_, V_ = range(5)
        JOBS = []
        for q in range(2):
            JOBS += [((n, q), "v") for n in ("TT", "T", "MT", "RBT", "RKT")]
        for q in range(2):
            JOBS += [((n, q), "s") for n in ("tokB", "tokK", "tokV")]
        for n in LEVELS[1:]:
            JOBS += [(("Y", n, q), "s") for q in range(2)]
            JOBS += [((z, n, q), "v") for q in range(2) for z in (("Z", "ZT") if n != LEVELS[-1] else ("ZT",))]
        for n in ("tokA", "UV", "W", "U"):
            JOBS += [((n, q), "s") for q in range(2)]
        for q in range(2):
            JOBS += [(("BW", q), "v"), (("RW", q), "v"), (("D", q), "s")]
        JOBS += [(("S", n), "v") for n in range(1, NCH)]
        RING = [name for name, _ in JOBS]
        RING_BANKS = 4
        RING_INDEX = {name: n for n, name in enumerate(RING)}
        READER = dict(JOBS)
        READS = {}
        for e in "vs":
            for n, name in enumerate(x for x in RING if READER[x] == e):
                READS[name] = n + 1
        RING_READS = {e: sum(READER[x] == e for x in RING) for e in "vs"}

        def ring_bank(name):
            return bank(RING_INDEX[name] % RING_BANKS)

        def ring_free(pe, i, name):
            n = RING_INDEX[name]
            if n >= RING_BANKS:
                last = RING[n - RING_BANKS]
                pe.wait_ge(g("bank_read_" + READER[last]), taken(i, last))

        def ring_full(pe, mm, name):
            mm.then_inc(g("bank_full"), 1)

        def full(eng, i, name):
            eng.wait_ge(g("bank_full"), i * len(RING) + (RING_INDEX[name] + 1))

        def take(eng, i, name):
            full(eng, i, name)
            return ring_bank(name)

        def taken(i, name):
            return i * RING_READS[READER[name]] + READS[name]

        def was_taken(pe, i, name):
            pe.wait_ge(g("bank_read_" + READER[name]), taken(i, name))

        def quad(t, q):
            return t[:, 4 * q:4 * q + 4, :]

        def blocks(bk):
            return bk.rearrange("p (c n) -> p c n", n=P)

        def masked(c):
            return const(c).unsqueeze(1).broadcast_to([P, 4, P])

        def features_vector(dve, i, chain, between):
            chain(nc.vector.tensor_copy(PV[:, :], VEC[:, bass.ds(i * 10 + V_PAIR, 10)]))
            w0, a0, kk, ka, rk, lg, lb, mr, mk, mv = (PV[:, n:n + 1] for n in range(10))
            for n, (x, mu) in enumerate(((XK, mk), (XV, mv), (XR, mr))):
                c = (4, 8, 0)[n]
                last = SHIFT[:, bass.ds(i + c, 1), :].rearrange("p a n -> p (a n)")
                ins = shift(dve, chain, x, i + (12 + c), last, mu)
                ins.then_inc(g("shifted"), 1)
                dve.wait_ge(g("shifted"), i * 3 + (n + 1))
            between(0)
            dve.wait_ge(g("gates"), i + 1)
            chain(nc.vector.tensor_scalar(LW, LW, -math.exp(-0.5), None, ALU.mult))
            chain(nc.vector.tensor_tensor_scan(CUM[:, 0:SEQ], const(C_KEEP, SEQ), LW[:, 0:SEQ], 0.0,
                                               ALU.mult, ALU.add))
            cum = CUM[:, 0:SEQ].rearrange("p (c n) -> p c n", n=CH)
            dd = DD[:, 0:SEQ].rearrange("p (c n) -> p c n", n=CH)
            chain(nc.vector.tensor_tensor(dd, cum, cum[:, :, CH // 2 - 1:CH // 2].broadcast_to([P, NCH, CH]), ALU.subtract))
            nc.vector.tensor_tensor(GAIN[:, 0:NCH - 1].unsqueeze(2), dd[:, 0:NCH - 1, CH - 1:CH],
                                    cum[:, 1:NCH, CH // 2 - 1:CH // 2], ALU.add)
            nc.vector.tensor_copy(GAIN[:, NCH - 1:NCH].unsqueeze(2), dd[:, NCH - 1:NCH, CH - 1:CH])
            nc.vector.tensor_tensor(E3[:, 0:SEQ], DD[:, 0:SEQ], LW[:, 0:SEQ], ALU.subtract).then_inc(g("exponents"), 1)
            chain(nc.vector.tensor_scalar(K2, AG, 1.0, ka, ALU.subtract, ALU.mult))
            chain(nc.vector.scalar_tensor_tensor(out=K2, in0=K2, scalar=1.0, in1=XK, op0=ALU.add, op1=ALU.mult))
            nc.vector.scalar_tensor_tensor(out=BO, in0=XR, scalar=rk, in1=K2, op0=ALU.mult,
                                           op1=ALU.mult).then_inc(g("rk_ready"), 1)
            between(1)
            dve.wait_ge(g("kk_norm"), i + 1)
            chain(nc.vector.tensor_scalar(T1, T1, 1e-12, None, ALU.max))
            chain(nc.vector.reciprocal(T1, T1))
            chain(nc.vector.tensor_tensor(KK, KK, T1, ALU.mult))
            chain(nc.vector.tensor_tensor(BB, KK, AG, ALU.mult))
            between(2)
            dve.wait_ge(g("decays"), i + 1)
            for n, (x, e) in enumerate(((KK, E3), (BB, E2), (K2, E2))):
                for h in range(2):
                    rows = slice(64 * h, 64 * h + 64)
                    ins = nc.vector.tensor_tensor(BD[n][rows, :, 64 * h:64 * h + 64], by_chunk(x, rows),
                                                  by_chunk(e, rows), ALU.mult)
            ins.then_inc(g("bd_ready"), 1)
            dve.wait_ge(g("rk_summed"), i + 1)
            nc.vector.tensor_tensor(halves(BO), accv(0), halves(XV), ALU.mult).then_inc(g("bonus"), 1)

        def by_chunk(x, rows):
            return x[rows, 0:SEQ].rearrange("p (c n) -> p c n", n=CH)

        def features_pool(pool, i):
            pool.wait_ge(g("shifted"), i * 3 + 3)
            pool.wait_ge(g("decays"), i + 1)
            pool.wait_ge(g("k_multiplied"), i * 2 * PAGES + 12)
            for h in range(2):
                rows = slice(64 * h, 64 * h + 64)
                pool.tensor_tensor(BD[R_][rows, :, 64 * h:64 * h + 64], by_chunk(XR, rows), by_chunk(E1, rows),
                                   ALU.mult).then_inc(g("r_blocks"), 1)
                pool.wait_ge(g("r_blocks"), i * 2 + (h + 1))

        def features_scalar(act, i):
            nc.scalar.activation(PVS[:, :], VEC[:, bass.ds(i * 10 + V_PAIR, 10)], ACT.Copy).then_inc(g("pair_vectors"), 1)
            act.wait_ge(g("pair_vectors"), i + 1)
            act.wait_ge(g("lora_done"), i + 1)
            nc.scalar.activation(halves(LW), accv(0), ACT.Sigmoid, bias=PVS[:, 0:1])
            nc.scalar.activation(halves(AG), accv(1), ACT.Sigmoid, bias=PVS[:, 1:2]).then_inc(g("gates"), 1)
            nc.scalar.activation(halves(GG), accv(2), ACT.Copy).then_inc(g("g_ready"), 1)
            act.wait_ge(g("shifted"), i * 3 + 1)
            nc.scalar.activation(KK, XK, ACT.Copy, scale=PVS[:, 2:3]).then_inc(g("kk_scaled"), 1)
            act.wait_ge(g("kk_scaled"), i + 1)
            nc.scalar.activation(T1, KK, ACT.Square).then_inc(g("kk_squared"), 1)
            act.wait_ge(g("shifted"), i * 3 + 2)
            for h in range(2):
                rows = slice(64 * h, 64 * h + 64)
                ins = nc.scalar.activation(BD[V_][rows, :, 64 * h:64 * h + 64], by_chunk(XV, rows), ACT.Copy)
            ins.then_inc(g("v_blocks"), 1)
            act.wait_ge(g("kk_summed"), i + 1)
            nc.scalar.activation(halves(T1), accv(0), ACT.Sqrt).then_inc(g("kk_norm"), 1)
            act.wait_ge(g("exponents"), i + 1)
            nc.scalar.activation(E1[:, 0:SEQ], DD[:, 0:SEQ], ACT.Exp)
            nc.scalar.activation(E2[:, 0:SEQ], DD[:, 0:SEQ], ACT.Exp, scale=-1.0)
            nc.scalar.activation(GAIN[:, :], GAIN[:, :], ACT.Exp)
            nc.scalar.activation(E3[:, 0:SEQ], E3[:, 0:SEQ], ACT.Exp).then_inc(g("decays"), 1)

        def features_tensor(pe, i):
            pe.wait_ge(g("lora_in_sbuf"), i * 32 + 32)
            pe.wait_ge(g("lora_act"), 1)
            for a in range(2):
                cols = slice(HALF * a, HALF * a + HALF)
                nc.tensor.matmul(acc[0][:, a, 0:HALF], LORA[0:64, :], XWA[0:64, cols], start=True, stop=True)
                nc.tensor.matmul(acc[1][:, a, 0:HALF], LORA[64:P, :], XWA[64:P, cols], start=True, stop=True)
                mm = nc.tensor.matmul(acc[2][:, a, 0:HALF], LG2[:, :], XSG[:, cols], start=True, stop=True)
            mm.then_inc(g("lora_done"), 1)
            pe.wait_ge(g("kk_squared"), i + 1)
            pe.wait_ge(g("gates"), i + 1)
            for a in range(2):
                mm = nc.tensor.matmul(acc[0][:, a, 0:HALF], const(C_HEAD), T1[:, HALF * a:HALF * a + HALF], start=True, stop=True)
            mm.then_inc(g("kk_summed"), 1)
            pe.wait_ge(g("kk_norm"), i + 1)
            pe.wait_ge(g("rk_ready"), i + 1)
            for a in range(2):
                mm = nc.tensor.matmul(acc[0][:, a, 0:HALF], const(C_HEAD), BO[:, HALF * a:HALF * a + HALF], start=True, stop=True)
            mm.then_inc(g("rk_summed"), 1)

        def products(pe, i, name, lhs, rhs):
            ring_free(pe, i, name)
            for c in range(4):
                mm = nc.tensor.matmul(ring_bank(name)[:, P * c:P * c + P], lhs(c), rhs(c), start=True, stop=True)
            ring_full(pe, mm, name)

        def turned(pe, i, name, src):
            ring_free(pe, i, name)
            for c in range(4):
                mm = nc.tensor.transpose(ring_bank(name)[:, P * c:P * c + P], src(c), const(C_ID))
            ring_full(pe, mm, name)

        def of(t, q):
            return lambda c: t[:, 4 * q + c, :]

        def chunk_products_tensor(pe, i):
            pe.wait_ge(g("bonus"), i + 1)
            pe.wait_ge(g("g_ready"), i + 1)
            pe.wait_ge(g("bd_ready"), i + 1)
            for q in range(2):
                for name, a, b in (("TT", B_, A_), ("T", A_, B_), ("MT", K_, A_), ("RBT", B_, R_), ("RKT", K_, R_)):
                    if name == "RBT":
                        pe.wait_ge(g("r_blocks"), i * 2 + 2)
                    products(pe, i, (name, q), of(BD[a], q), of(BD[b], q))

        def tokens_tensor(pe, i):
            pe.wait_ge(g("v_blocks"), i + 1)
            for q in range(2):
                for name, n in (("tokB", B_), ("tokK", K_), ("tokV", V_)):
                    turned(pe, i, (name, q), of(BD[n], q))

        def level_begin_tensor(pe, i, l):
            for q in range(2):
                pe.wait_ge(g("level_masked"), i * 10 + (2 * l + q + 1))
                was_taken(pe, i, ("ZT", LEVELS[l], q) if l else ("T", q))
                products(pe, i, ("Y", LEVELS[l + 1], q), of(EE, q), of(PP, q))

        def level_end_tensor(pe, i, l, q):
            n = LEVELS[l + 1]
            was_taken(pe, i, ("Y", n, q))
            if l == 0:
                pe.wait_ge(g("turned_begun"), i * 2 + (q + 1))
            if n != LEVELS[-1]:
                products(pe, i, ("Z", n, q), of(PT, q), of(YY, q))
            products(pe, i, ("ZT", n, q), of(YY, q), of(PT, q))

        def solve_tensor(pe, i, part):
            for q in range(2):
                if part == 0:
                    turned(pe, i, ("tokA", q), of(BD[A_], q))
                if part == 1:
                    was_taken(pe, i, ("tokV", q))
                    products(pe, i, ("UV", q), of(MT, q), of(TK[V_], q))
                if part == 2:
                    was_taken(pe, i, ("ZT", LEVELS[-1], q))
                    was_taken(pe, i, ("tokA", q))
                    products(pe, i, ("W", q), of(PT, q), of(EE, q))
                if part == 3:
                    was_taken(pe, i, ("UV", q))
                    products(pe, i, ("U", q), of(PT, q), of(YY, q))
                if part == 4:
                    was_taken(pe, i, ("W", q))
                    products(pe, i, ("BW", q), of(TT, q), of(TK[B_], q))
                    products(pe, i, ("RW", q), of(TT, q), of(RBT, q))
                    was_taken(pe, i, ("U", q))
                    ring_free(pe, i, ("D", q))
                    for c in range(4):
                        out = ring_bank(("D", q))[:, P * c:P * c + P]
                        nc.tensor.matmul(out, of(TK[B_], q)(c), of(MT, q)(c), start=True, stop=False)
                        mm = nc.tensor.matmul(out, of(TK[K_], q)(c), of(TK[V_], q)(c), start=False, stop=True)
                    ring_full(pe, mm, ("D", q))

        def outputs_tensor(pe, i, q):
            if q == 0:
                pe.wait_ge(g("exped"), i * 8 + 8)
            for c in range(4):
                out = bank(4 + q)[:, P * c:P * c + P]
                nc.tensor.matmul(out, of(MT, q)(c), of(RBT, q)(c), start=c == 0, stop=False, skip_group_check=True)
                mm = nc.tensor.matmul(out, of(TK[V_], q)(c), of(RKT, q)(c), start=False,
                                      stop=q == 0 and c == 0, skip_group_check=True)

        def chain_tensor(pe, i, n):
            was_taken(pe, i, ("S", n - 1) if n > 1 else ("D", 0))
            if n == 1:
                pe.wait_ge(g("first_state"), i + 1)
            if n % 4 == 0 or n == 1:
                was_taken(pe, i, ("RW", n // 4))
            if n == 4:
                was_taken(pe, i, ("D", 1))
            ring_free(pe, i, ("S", n))
            mm = nc.tensor.matmul(ring_bank(("S", n))[:, 0:P], PP[:, n, :], BD[A_][:, n, :], start=True, stop=True)
            ring_full(pe, mm, ("S", n))
            mm = nc.tensor.matmul(bank(4 + n // 4)[:, P * (n % 4):P * (n % 4) + P], BD[A_][:, n, :], BD[R_][:, n, :],
                                  start=False, stop=True, skip_group_check=True)
            if n % 4 == 3:
                mm.then_inc(g("out_quad"), 1)

        def chunk_products_vector(dve, i, chain):
            for q in range(2):
                for name, out, mask in ((("TT", q), TT, C_STRICT), (("T", q), None, None), (("MT", q), MT, C_STRICT),
                                        (("RBT", q), RBT, C_INCL), (("RKT", q), RKT, C_INCL)):
                    src = blocks(take(dve, i, name))
                    if out is None:
                        chain(nc.vector.tensor_tensor(quad(PP, q), src, masked(C_LOW1), ALU.mult))
                        ins = nc.vector.tensor_tensor(quad(PP, q), masked(C_ID), quad(PP, q), ALU.subtract)
                    else:
                        ins = nc.vector.tensor_tensor(quad(out, q), src, masked(mask), ALU.mult)
                    ins.then_inc(g("bank_read_v"), 1)

        def level_vector(dve, i, l, q):
            n = LEVELS[l + 1]
            for z, t in (("Z", PP), ("ZT", PT)):
                if (z, n, q) in RING_INDEX:
                    src = blocks(take(dve, i, (z, n, q)))
                    if z == "Z":
                        full(dve, i, ("ZT", n, q))
                    nc.vector.tensor_tensor(quad(t, q), quad(t, q), src, ALU.subtract).then_inc(g("bank_read_v"), 1)

        def solve_vector(dve, i, q):
            src = blocks(take(dve, i, ("BW", q)))
            nc.vector.tensor_tensor(quad(PP, q), masked(C_ID), src, ALU.subtract).then_inc(g("bank_read_v"), 1)
            src = blocks(take(dve, i, ("RW", q)))
            nc.vector.tensor_tensor(quad(BD[R_], q), quad(BD[R_], q), src, ALU.subtract).then_inc(g("bank_read_v"), 1)

        def chain_begin_vector(dve, i):
            dve.wait_ge(g("bank_read_s"), taken(i, ("D", 0)))
            full(dve, i, ("tokA", 1))
            nc.vector.tensor_copy(BD[A_][:, 1, :], BD[K_][:, 0, :]).then_inc(g("first_state"), 1)

        def chain_vector(dve, i, n):
            src = take(dve, i, ("S", n))[:, 0:P]
            if n == 4:
                dve.wait_ge(g("bank_read_s"), taken(i, ("D", 1)))
            out = BD[A_][:, n + 1, :] if n + 1 < NCH else LAST[:, :]
            nc.vector.scalar_tensor_tensor(out=out, in0=src, scalar=GAIN[:, n:n + 1], in1=BD[K_][:, n, :],
                                           op0=ALU.mult, op1=ALU.add).then_inc(g("bank_read_v"), 1)

        def outputs_scalar(act, i, q):
            act.wait_ge(g("out_quad"), i * 2 + (q + 1))
            for h in range(2):
                rows = slice(64 * h, 64 * h + 64)
                ins = nc.scalar.activation(by_chunk(OT, rows)[:, 4 * q:4 * q + 4, :],
                                           blocks(bank(4 + q))[rows, :, 64 * h:64 * h + 64], ACT.Copy)
            ins.then_inc(g("out_read"), 1)

        def copy_out_scalar(act, i, name, out, scale=1.0):
            src = blocks(take(act, i, name))
            nc.scalar.activation(out, src, ACT.Copy, scale=scale).then_inc(g("bank_read_s"), 1)

        def tokens_scalar(act, i):
            for q in range(2):
                for name, n in (("tokB", B_), ("tokK", K_), ("tokV", V_)):
                    copy_out_scalar(act, i, (name, q), quad(TK[n], q))

        def level_scalar(act, i, l):
            for q in range(2):
                if l:
                    full(act, i, ("ZT", LEVELS[l], q))
                copy_out_scalar(act, i, ("Y", LEVELS[l + 1], q), quad(YY, q))

        def solve_scalar(act, i, part):
            for q in range(2):
                if part == 0:
                    full(act, i, ("Y", LEVELS[-1], q))
                    copy_out_scalar(act, i, ("tokA", q), quad(EE, q))
                if part == 1:
                    full(act, i, ("ZT", LEVELS[-1], q))
                    copy_out_scalar(act, i, ("UV", q), quad(YY, q), -1.0)
                if part == 2:
                    act.wait_ge(g("level_masked"), i * 10 + 10)
                    copy_out_scalar(act, i, ("W", q), quad(TT, q))
                if part == 3:
                    full(act, i, ("UV", q))
                    copy_out_scalar(act, i, ("U", q), quad(MT, q))
                if part == 4:
                    src = blocks(take(act, i, ("D", q)))
                    for c in range(4):
                        n = 4 * q + c
                        ins = nc.scalar.activation(BD[K_][:, n, :], src[:, c, :], ACT.Copy, scale=GAIN[:, n:n + 1])
                    ins.then_inc(g("bank_read_s"), 1)

        def level_pool(pool, i, l):
            for q in range(2):
                if l == 0:
                    was_taken(pool, i, ("TT", q))
                else:
                    full(pool, i, ("Y", LEVELS[l], q))
                pool.tensor_tensor(quad(EE, q), quad(TT, q), masked(C_LEV + P * (l + 1)), ALU.mult)\
                    .then_inc(g("level_masked"), 1)
            if l == 0:
                for q in range(2):
                    pool.tensor_tensor(quad(PT, q), quad(TT, q), masked(C_LEV), ALU.mult).then_inc(g("pool_link"), 1)
                    pool.wait_ge(g("pool_link"), i * 2 + (q + 1))
                    pool.tensor_tensor(quad(PT, q), masked(C_ID), quad(PT, q), ALU.subtract).then_inc(g("turned_begun"), 1)

        def step_vector(dve, i, chain, part):
            s3 = lambda t: t.rearrange("p (b v) -> p b v", v=64)
            SS, PD, VB = SCR[:, 1, 0:SEQ], SCR[:, 2, 0:SEQ], SCR[:, 3, 0:SEQ]
            unit = ID2[:, :].unsqueeze(1).broadcast_to([P, DEC, 64])

            def per_key(x):
                return x[:, SEQ:TOK].unsqueeze(2).broadcast_to([P, DEC, 64])
            if part == 0:
                dve.wait_ge(g("state_in"), i * 16 + 16)
                nc.vector.tensor_tensor(s3(PD), s3(SS), per_key(KK), ALU.mult).then_inc(g("step_terms"), 1)
            if part == 1:
                nc.vector.tensor_tensor(s3(VB), unit, per_key(XV), ALU.mult).then_inc(g("step_terms"), 1)
            if part == 2:
                dve.wait_ge(g("decay_d"), i + 1)
                chain(nc.vector.tensor_tensor(s3(SS), s3(SS), per_key(T1), ALU.mult))
            if part == 3:
                dve.wait_ge(g("step_sums"), i * 3 + 1)
                nc.vector.tensor_tensor(s3(PD), s3(bank(6)), per_key(BB), ALU.mult).then_inc(g("step_taken"), 1)
                dve.wait_ge(g("step_taken"), i * 2 + 1)
                chain(nc.vector.tensor_tensor(SS, SS, PD, ALU.subtract))
            if part == 4:
                dve.wait_ge(g("step_sums"), i * 3 + 2)
                nc.vector.tensor_tensor(s3(VB), s3(bank(6)), per_key(K2), ALU.mult).then_inc(g("step_taken"), 1)
                dve.wait_ge(g("step_taken"), i * 2 + 2)
                nc.vector.tensor_tensor(SS, SS, VB, ALU.add).then_inc(g("step_state"), 1)
            if part == 5:
                dve.wait_ge(g("step_state"), i + 1)
                nc.vector.tensor_tensor(s3(PD), s3(SS), per_key(XR), ALU.mult).then_inc(g("step_read"), 1)
            if part == 6:
                dve.wait_ge(g("step_sums"), i * 3 + 3)
                chain(nc.vector.tensor_tensor(s3(VB), s3(bank(6)), unit, ALU.mult))
                nc.vector.reduce_sum(OT[:, SEQ:TOK], s3(VB), AX.X).then_inc(g("o_ready"), 1)

        def step_tensor(pe, i, part):
            PD, VB = SCR[:, 2, 0:SEQ], SCR[:, 3, 0:SEQ]
            if part == 0:
                pe.wait_ge(g("step_terms"), i * 2 + 1)
                pe.wait_ge(g("head_out"), i + 1)
            if part == 1:
                pe.wait_ge(g("step_terms"), i * 2 + 2)
                pe.wait_ge(g("step_taken"), i * 2 + 1)
            if part == 2:
                pe.wait_ge(g("step_read"), i + 1)
            nc.tensor.matmul(bank(6), const(C_HEAD), VB if part == 1 else PD, start=True, stop=True)\
                .then_inc(g("step_sums"), 1)

        def step_scalar(act, i):
            act.wait_ge(g("pv_done"), i + 1)
            act.dma_start(SCR[:, 1, 0:SEQ], state_in[bass.ds(i, 1), :, :].rearrange("a p n -> (a p) n"))\
                .then_inc(g("state_in"), 16)
            nc.scalar.activation(T1[:, SEQ:TOK], LW[:, SEQ:TOK], ACT.Exp).then_inc(g("decay_d"), 1)

        def output_vector(dve, i, chain):
            dve.wait_ge(g("gn_mean"), i + 1)
            chain(nc.vector.scalar_tensor_tensor(out=halves(OT), in0=accv(0), scalar=-1.0 / 64, in1=halves(OT),
                                                 op0=ALU.mult, op1=ALU.add))
            nc.vector.tensor_tensor(T1, OT, OT, ALU.mult).then_inc(g("gn_squared"), 1)
            dve.wait_ge(g("gn_std"), i + 1)
            chain(nc.vector.reciprocal(T1, T1))
            chain(nc.vector.tensor_tensor(OT, OT, T1, ALU.mult))
            chain(nc.vector.tensor_scalar(OT, OT, PV[:, 5:6], PV[:, 6:7], ALU.mult, ALU.add))
            chain(nc.vector.tensor_tensor(OT, OT, BO, ALU.add))
            nc.vector.tensor_tensor(Y[:, bass.ds(i + 4, 1), :].rearrange("p a n -> p (a n)"), OT, GG,
                                    ALU.mult).then_inc(g("pair_out"), 1)

        def output_tensor(pe, i, part):
            if part == 1:
                pe.wait_ge(g("gn_squared"), i + 1)
                for a in range(2):
                    mm = nc.tensor.matmul(acc[1][:, a, 0:HALF], const(C_HEAD), T1[:, HALF * a:HALF * a + HALF],
                                          start=True, stop=True)
                mm.then_inc(g("gn_var"), 1)
                return
            pe.wait_ge(g("o_ready"), i + 1)
            was_taken(pe, i, ("S", NCH - 1))
            pe.wait_ge(g("out_read"), i * 2 + 2)
            was_taken(pe, i, ("D", 1))
            for a in range(2):
                mm = nc.tensor.matmul(acc[0][:, a, 0:HALF], const(C_HEAD), OT[:, HALF * a:HALF * a + HALF], start=True, stop=True)
            mm.then_inc(g("gn_mean"), 1)

        def output_scalar(act, i):
            act.wait_ge(g("gn_var"), i + 1)
            nc.scalar.activation(halves(T1), accv(1), ACT.Sqrt, bias=EPS[:, 3:4], scale=1.0 / 64).then_inc(g("gn_std"), 1)

        D_BANK = 7
        QUARTER = [range(4 * n, 4 * n + 4) for n in range(4)]
        LINKS = 59
        N_LEVELS = len(LEVELS) - 1

        def turn_pool(pool, i):
            b = 2 * i
            decode_query_pool(pool, b)
            for n in range(3):
                decode_pages_pool(pool, b, QUARTER[n])
            features_pool(pool, i)
            decode_pages_pool(pool, b, QUARTER[3])
            level_pool(pool, i, 0)
            decode_query_pool(pool, b + 1)
            for l in range(1, N_LEVELS):
                level_pool(pool, i, l)
                decode_pages_pool(pool, b + 1, QUARTER[l - 1])
            pool.wait_ge(g("d_out"), 2 * i + 3)

        def turn_tensor(pe, i):
            b = 2 * i
            decode_query_tensor(pe, b, D_BANK, False)
            features_tensor(pe, i)
            chunk_products_tensor(pe, i)
            decode_softmax_tensor(pe, b, D_BANK, 0)
            tokens_tensor(pe, i)
            decode_softmax_tensor(pe, b, D_BANK, 1)
            for l in range(N_LEVELS):
                level_begin_tensor(pe, i, l)
                if l == 0:
                    attention_v_tensor(pe, i)
                    decode_softmax_tensor(pe, b, D_BANK, 3)
                if l < 4:
                    attention_logits_tensor(pe, i, l)
                level_end_tensor(pe, i, l, 0)
                if l:
                    attention_turn_tensor(pe, i, l - 1)
                level_end_tensor(pe, i, l, 1)
                if l == 0:
                    decode_query_tensor(pe, b + 1, D_BANK, True)
                else:
                    if l == 1:
                        pe.wait_ge(g("q_rows"), b + 2)
                    decode_values_tensor(pe, b, D_BANK, QUARTER[l - 1])
            solve_tensor(pe, i, 0)
            solve_tensor(pe, i, 1)
            attention_values_tensor(pe, i)
            decode_softmax_tensor(pe, b + 1, D_BANK, 0)
            solve_tensor(pe, i, 2)
            decode_softmax_tensor(pe, b + 1, D_BANK, 1)
            solve_tensor(pe, i, 3)
            solve_tensor(pe, i, 4)
            outputs_tensor(pe, i, 0)
            decode_softmax_tensor(pe, b + 1, D_BANK, 3)
            outputs_tensor(pe, i, 1)
            for n in range(1, NCH):
                chain_tensor(pe, i, n)
                if n in (1, 4, 7):
                    decode_values_tensor(pe, b + 1, D_BANK, QUARTER[n // 3])
                if n in (2, 4, 6):
                    step_tensor(pe, i, n // 2 - 1)
            output_tensor(pe, i, 0)
            output_tensor(pe, i, 1)
            decode_values_tensor(pe, b + 1, D_BANK, QUARTER[3])
            pe.wait_ge(g("d_out"), 2 * i + 3)

        def turn_scalar(act, i):
            b = 2 * i
            act.dma_start(LORA[:, :], lora[bass.ds(i, 1), :, :].rearrange("a p n -> (a p) n")).then_inc(g("lora_in_sbuf"), 16)
            act.dma_start(LG2[:, :], g2[bass.ds(i, 1), :, :].rearrange("a p n -> (a p) n")).then_inc(g("lora_in_sbuf"), 16)
            decode_query_scalar(act, b, D_BANK)
            features_scalar(act, i)
            attention_begin_scalar(act, i)
            tokens_scalar(act, i)
            decode_softmax_scalar(act, b)
            for l in range(N_LEVELS):
                level_scalar(act, i, l)
                if l == 0:
                    attention_v_scalar(act, i)
                if l < 4:
                    attention_exp_scalar(act, i, l)
                if l:
                    attention_turn_scalar(act, i, l - 1)
                if l == 0:
                    decode_query_scalar(act, b + 1, D_BANK)
            solve_scalar(act, i, 0)
            solve_scalar(act, i, 1)
            attention_out_scalar(act, i)
            step_scalar(act, i)
            solve_scalar(act, i, 2)
            decode_softmax_scalar(act, b + 1)
            solve_scalar(act, i, 3)
            solve_scalar(act, i, 4)
            outputs_scalar(act, i, 0)
            outputs_scalar(act, i, 1)
            act.wait_ge(g("bank_read_v"), taken(i, ("S", NCH - 1)))
            act.dma_start(wkv_out[bass.ds(i, 1), :, :].rearrange("a p n -> (a p) n"), LAST[:, :]).then_inc(g("states_out"), 16)
            act.wait_ge(g("step_state"), i + 1)
            act.dma_start(wkv_s_out[bass.ds(i, 1), :, :].rearrange("a p n -> (a p) n"), SCR[:, 1, 0:SEQ]).then_inc(g("states_out"), 16)
            output_scalar(act, i)
            act.wait_ge(g("states_out"), i * 32 + 32)
            act.wait_ge(g("d_out"), 2 * i + 3)

        def turn_vector(dve, i):
            chain = Chain(dve, g("dve_turn"), i, LINKS)
            b = 2 * i
            features_vector(dve, i, chain, lambda n: decode_pages_vector(dve, b, QUARTER[n]))
            chunk_products_vector(dve, i, chain)
            decode_pages_vector(dve, b, QUARTER[3])
            decode_softmax_vector(dve, b, D_BANK, chain, 0)
            decode_softmax_vector(dve, b, D_BANK, chain, 1)
            decode_softmax_vector(dve, b, D_BANK, chain, 2)
            for l in range(N_LEVELS):
                if l == 0:
                    decode_softmax_vector(dve, b, D_BANK, chain, 3)
                if l < 4:
                    attention_max_vector(dve, i, l, chain)
                level_vector(dve, i, l, 0)
                if l == 0:
                    decode_softmax_vector(dve, b, D_BANK, chain, 4)
                level_vector(dve, i, l, 1)
                if l < 4:
                    attention_weights_vector(dve, i, l, chain)
                if l:
                    decode_pages_vector(dve, b + 1, QUARTER[l - 1])
            decode_values_vector(dve, b, D_BANK, chain)
            decode_softmax_vector(dve, b + 1, D_BANK, chain, 0)
            decode_softmax_vector(dve, b + 1, D_BANK, chain, 1)
            decode_softmax_vector(dve, b + 1, D_BANK, chain, 2)
            solve_vector(dve, i, 0)
            decode_softmax_vector(dve, b + 1, D_BANK, chain, 3)
            solve_vector(dve, i, 1)
            chain_begin_vector(dve, i)
            decode_softmax_vector(dve, b + 1, D_BANK, chain, 4)
            step_vector(dve, i, chain, 0)
            for n in range(1, NCH):
                chain_vector(dve, i, n)
                if n < NCH - 1:
                    step_vector(dve, i, chain, n)
            output_vector(dve, i, chain)
            decode_values_vector(dve, b + 1, D_BANK, chain)
            chain.end()

        MIX_ORDER = list(range(DA_HEADS, DC)) + list(range(DA_HEADS))

        def mixed_scalar(act):
            act.wait_ge(stored, 3 * 16)
            for c in range(DA_HEADS):
                nc.scalar.activation(SCR[:, c, :], Y[:, c, :], ACT.Square).then_inc(g("m_squared"), 1)
            for c in range(DA_HEADS, DC):
                nc.scalar.activation(MH[:, c, :], Y[:, c, :], ACT.Copy).then_inc(g("mix_hi"), 1)
            split_high(act, outp, 0, 0)
            for c in range(DA_HEADS):
                act.wait_ge(g("m_summed"), c + 1)
                nc.scalar.activation(halves(SCR[:, c, :]), accv(c), ACT.Sqrt, bias=EPS[:, 4:5],
                                     scale=float(D_MODEL // P)).then_inc(g("m_std"), 1)
            for c in range(DA_HEADS):
                act.wait_ge(g("m_scaled"), c + 1)
                nc.scalar.activation(MH[:, c, :], Y[:, c, :], ACT.Copy).then_inc(g("mix_hi"), 1)

        def mixed_tensor(pe):
            for c in range(DA_HEADS):
                pe.wait_ge(g("m_squared"), c + 1)
                for a in range(2):
                    mm = nc.tensor.matmul(acc[c][:, a, 0:HALF], MEAN[:, :], SCR[:, c, HALF * a:HALF * a + HALF],
                                          start=True, stop=True)
                mm.then_inc(g("m_summed"), 1)

        def mixed_vector(dve):
            chain = Chain(dve, g("dve_mixed"))
            chain(nc.vector.tensor_scalar(VEC[:, V_SUB:V_SUB + 1], VEC[:, V_SUB:V_SUB + 1], 1.0 - LAM_INIT, None, ALU.mult))
            for n, c in enumerate(MIX_ORDER):
                if c < DA_HEADS:
                    dve.wait_ge(g("m_std"), c + 1)
                    chain(nc.vector.reciprocal(SCR[:, c, :], SCR[:, c, :]))
                    nc.vector.scalar_tensor_tensor(out=Y[:, c, :], in0=Y[:, c, :], scalar=VEC[:, V_SUB:V_SUB + 1],
                                                   in1=SCR[:, c, :], op0=ALU.mult, op1=ALU.mult).then_inc(g("m_scaled"), 1)
                dve.wait_ge(g("mix_hi"), n + 1)
                nc.vector.tensor_tensor(ML[:, c, :], Y[:, c, :], MH[:, c, :].bitcast(f32), ALU.subtract)\
                    .then_inc(g("mix_ready"), 1)
                if n == DC - DA_HEADS - 1:
                    split_low(dve, outp, 0, 0)

        block = ctx.enter_context(nc.Block())

        @block.sync
        def _(sp):

            def stream(pr, src):
                load_weights(sp, pr, 0, lambda i, b: src(0, b))
                if pr.times > 1:
                    with sp.Fori(1, pr.times) as i:
                        load_weights(sp, pr, i, src)

            def by_pair(w):
                return lambda i, b: w[bass.ds(i * 2 + b, 1), :, :].rearrange("a p (k n) -> p (a k) n", n=2 * P)

            def down(w):
                def src(i, b):
                    k0, nk = DOWN_BODY[b][:2]
                    return w[bass.ds(i * 2 + b // 4, 1), :, k0 * 2 * P:(k0 + nk) * 2 * P]\
                        .rearrange("a p (k n) -> p (a k) n", n=2 * P)
                return src

            stream(up_a, by_pair(gu_a))
            stream(dn_a, down(down_a))
            stream(inp, by_pair(w_in))
            stream(inp_tail, lambda i, b: w_in[12, :, :].rearrange("p (k n) -> p k n", n=2 * P))
            sp.wait_ge(slab_used, 2 * inp.block0)
            sp.dma_start(CONST[:, :], consts[:, 0:NCONST]).then_inc(g("consts_in"), 16)
            sp.dma_start(LAMV[:, :], lams).then_inc(g("small_in"), 16)
            sp.dma_start(SHIFT[:, :, :], shift_in).then_inc(g("small_in"), 16)
            sp.dma_start(TABLE[:, :], pages).then_inc(g("table_in"), 16)
            sp.wait_ge(x_ready, 2 * DC)
            sp.dma_start(Y[:, 6:8, :], consts[:, NCONST:NCONST + 2 * TOK].rearrange("p (a n) -> p a n", n=TOK))\
                .then_inc(g("small_in"), 16)
            projected(sp)
            sp.dma_start(hi_dram, XH[:, :, :].bitcast(f32)).then_inc(g("spilled"), 16)
            sp.dma_start(lo_dram, XL[:, :, :].bitcast(f32)).then_inc(g("spilled"), 16)
            sp.dma_start(v_out, PROJ[:, 8:12, :]).then_inc(stored, 16)
            sp.dma_start(shift_out, PROJ[:, 12:IN_CHUNKS, SEQ - 1:TOK]).then_inc(stored, 16)
            sp.wait_ge(g("table_in"), 16)
            decode_loads(sp)
            sp.wait_ge(g("roped"), 8)
            sp.dma_start(k_out, PROJ[:, 4:8, :]).then_inc(stored, 16)
            sp.wait_ge(g("d_out"), DEC + 1)
            stream(outp, by_pair(w_out))
            sp.dma_start(XH[:, :, :].bitcast(f32), hi_dram).then_inc(g("restored"), 16)
            sp.dma_start(XL[:, :, :].bitcast(f32), lo_dram).then_inc(g("restored"), 16)
            sp.wait_ge(stored, 3 * 16)
            stream(up_b, by_pair(gu_b))
            stream(dn_b, down(down_b))
            for c in range(DC):
                sp.wait_ge(x_hi, 3 * DC + c + 1)
                sp.dma_start(y_out[:, c, :], Y[:, c, :]).then_inc(stored, 16)
            sp.wait_ge(stored, 16 * (3 + DC))

        @block.gpsimd
        def _(pool):
            pool.memset(MEAN[:, :], 1.0 / D_MODEL).then_inc(consts_set, 1)
            for n, e in enumerate((4 * LN_EPS, LN_EPS, 4 * LN_EPS, GN_EPS, LN_EPS)):
                pool.memset(EPS[:, n:n + 1], e).then_inc(consts_set, 1)
            norm_pool(pool, 0)
            pool.wait_ge(g("small_in"), 48)
            prelude_pool(pool)
            pool.wait_ge(g("spilled"), 32)
            for n in range(5):
                pool.memset(BD[n][:, :, :], 0.0).then_inc(g("blocks_cleared"), 1)
            with pool.Fori(0, DA_HEADS) as i:
                turn_pool(pool, i)
            norm_pool(pool, 1)
            norm_pool(pool, 2)

        @block.scalar
        def _(act):
            for n in range(DC // 2):
                act.dma_start(Y[:, 2 * n:2 * n + 2, :], x_in[:, 2 * n:2 * n + 2, :]).then_inc(x_loaded[n], 16)
            act.dma_start(VEC[:, :], vecs).then_inc(tables_in, 16)
            act.wait_ge(consts_set, 6)
            split_high(act, up_a, 0, 0)
            for c in range(DC):
                act.wait_ge(x_loaded[c // 2], 16)
                nc.scalar.activation(XH[:, c, :], Y[:, c, :], ACT.Copy).then_inc(x_hi, 1)
            act.wait_ge(tables_in, 16)
            for k in range(1, 4):
                split_high(act, up_a, 0, k)
            gate_up(gate_up_scalar, act, up_a, 0)
            down_scalar(act, dn_a)
            norm_scalar(act, 0, inp)
            input_scalar(act)
            prelude_scalar(act)
            act.wait_ge(g("spilled"), 32)
            with act.Fori(0, DA_HEADS) as i:
                turn_scalar(act, i)
            mixed_scalar(act)
            for k in range(1, 4):
                split_high(act, outp, 0, k)
            for k in range(4):
                split_high(act, outp, 1, k)
            norm_scalar(act, 1, up_b)
            gate_up(gate_up_scalar, act, up_b, 1)
            down_scalar(act, dn_b)
            norm_scalar(act, 2, out=True)

        @block.vector
        def _(dve):
            split_low(dve, up_a, 0, 0)
            for c in range(DC):
                dve.wait_ge(x_hi, c + 1)
                nc.vector.tensor_tensor(XL[:, c, :], Y[:, c, :], XH[:, c, :].bitcast(f32),
                                        ALU.subtract).then_inc(x_ready, 1)
            dve.wait_ge(tables_in, 16)
            for k in range(1, 4):
                split_low(dve, up_a, 0, k)
            gate_up(gate_up_vector, dve, up_a, 0)
            down_vector(dve, dn_a)
            norm_vector(dve, 0, inp)
            with dve.Fori(1, inp.times) as i:
                for k in range(4):
                    split_low(dve, inp, i, k)
            for k in range(2):
                split_low(dve, inp_tail, 0, k)
            prelude_vector(dve)
            dve.wait_ge(g("spilled"), 32)
            dve.wait_ge(g("blocks_cleared"), 5)
            with dve.Fori(0, DA_HEADS) as i:
                turn_vector(dve, i)
            mixed_vector(dve)
            for k in range(1, 4):
                split_low(dve, outp, 0, k)
            dve.wait_ge(g("restored"), 32)
            for i in range(2):
                for k in range(4):
                    residual(dve, outp, i, k, 4 * i + k, ALPHA)
                    if i == 0:
                        split_low(dve, outp, 1, k)
            norm_vector(dve, 1, up_b)
            gate_up(gate_up_vector, dve, up_b, 1)
            down_vector(dve, dn_b)
            norm_vector(dve, 2, last=True)

        @block.tensor
        def _(pe):
            pe.wait_ge(consts_set, 6)
            gate_up_tensor(pe, up_a, 0)
            down_tensor(pe, dn_a, 0)
            norm_tensor(pe, 0)
            multiply(pe, inp, 0, XH, XL, (x_ready, DC))
            with pe.Fori(1, inp.times) as i:
                multiply(pe, inp, i, XH, XL)
            multiply(pe, inp_tail, 0, XH, XL)
            prelude_tensor(pe)
            pe.wait_ge(g("own_ready"), 1)
            with pe.Fori(0, DA_HEADS) as i:
                turn_tensor(pe, i)
            mixed_tensor(pe)
            pe.wait_ge(g("m_std"), DA_HEADS)
            multiply(pe, outp, 0, MH, ML, (g("mix_ready"), 0), MIX_ORDER)
            multiply(pe, outp, 1, MH, ML)
            norm_tensor(pe, 1)
            gate_up_tensor(pe, up_b, 2)
            down_tensor(pe, dn_b, 1)
            norm_tensor(pe, 2)


def constants():
    a = np.arange(P)
    t, s = a[None, :], a[:, None]
    head = t // CH == s // CH
    out = [t == s,
           (t // 64 == s // 64) & ((t % 64 + 32) % 64 == s % 64),
           np.where(s < t, NEG, 0.0),
           head & (s < t), head & (s <= t), head,
           (s % 2 == 1) & (t == s - 1)]
    for n in LEVELS:
        out.append(head & ((t // n) % 2 == 1) & (s // n == t // n - 1))
    keep = np.broadcast_to(np.arange(SEQ) % CH != 0, (P, SEQ))
    half = DA_QK // 2
    inv = np.float32(10000.0) ** (-np.arange(half, dtype=np.float32) / np.float32(half))
    pos = np.concatenate([np.arange(SEQ), np.full(DEC, PAST)]).astype(np.float32)
    ang = (pos[:, None] * inv.astype(np.float32)[None, :]).astype(np.float32).T
    cos = np.tile(np.cos(ang), (4, 1))
    sin = np.concatenate([-np.sin(ang), np.sin(ang)] * 2, 0)
    return np.concatenate([np.asarray(x, np.float32) for x in (*out, keep, cos, sin)], 1)


def kernel(**a):
    import concourse.bacc as bacc
    from concourse.bass_utils import run_bass_kernel_spmd

    def fm(v, n):
        return v.reshape(n, P).T

    x = np.concatenate([a["x_prompt"][0], a["x_sample"][:, 0]], 0).T.reshape(DC, P, TOK).transpose(1, 0, 2)

    def by_pair(w):
        return w[0].reshape(DC, P, -1, 2 * P).transpose(2, 1, 0, 3).reshape(-1, P, DC * 2 * P)

    def gate_up(w):
        return w[0].reshape(DC, P, 2, FC // 2, 2 * P).transpose(3, 2, 1, 0, 4).reshape(FC, P, DC * 2 * P)

    def down(w):
        return w[0].reshape(FC, P, DC // 2, 2 * P).transpose(2, 1, 0, 3).reshape(DC // 2, P, FC * 2 * P)

    mu = fm(a["rw_mu"], RC)
    cols = [fm(a[n], DC) for n in ("ln1_g", "ln1_b", "ln2_g", "ln2_b", "ln3_g", "ln3_b")]
    cols += [fm(a["da_subln_g"], 1), mu[:, 12:14]]
    per = [fm(a[n], 4) for n in ("rw_w0", "rw_a0", "rw_k_k", "rw_k_a", "rw_r_k", "rw_lnx_g", "rw_lnx_b")]
    for i in range(4):
        cols += [v[:, i:i + 1] for v in per] + [mu[:, i + 4 * n:i + 4 * n + 1] for n in range(3)]
    lam = np.concatenate([a[n][0] for n in ("da_lq1", "da_lk1", "da_lq2", "da_lk2")])
    lora = np.concatenate([a["rw_w2"][0], a["rw_a2"][0]], 0).reshape(P, 4, P).transpose(1, 0, 2)
    state = a["state_wkv"][0].reshape(DEC, 4, 2, 64, 64).transpose(1, 2, 4, 0, 3).reshape(4, P, DEC * 64)
    ins = {
        "x": x, "gate_up_a": gate_up(a["ffa_w_gu"]), "down_a": down(a["ffa_w_down"]), "w_in": by_pair(a["w_in"]),
        "w_out": by_pair(a["w_out"]), "gate_up_b": gate_up(a["ffb_w_gu"]), "down_b": down(a["ffb_w_down"]),
        "constants": constants(), "vectors": np.concatenate(cols, 1), "lambdas": np.broadcast_to(lam, (P, 256)),
        "lora": lora, "g2": a["rw_g2"][0].reshape(P, 4, P).transpose(1, 0, 2),
        "cache_k": a["cache_k"][0].reshape(POOL, PAGE, 512), "cache_v": a["cache_v"][0].reshape(POOL, PAGE, 512),
        "pages": a["page_table"].reshape(1, DEC * PAGES), "state": state,
        "shift": a["state_shift"][0, :, 0].T.reshape(RC, P, DEC).transpose(1, 0, 2),
    }
    ins = {k: np.ascontiguousarray(v) for k, v in ins.items()}
    outs = {"y": (P, DC, TOK), "k": (P, 4, TOK), "v": (P, 4, TOK), "wkv": (4, P, P),
            "shift_rows": (P, RC, TOK - SEQ + 1), "wkv_decode": (4, P, DEC * 64)}
    nc = bacc.Bacc("TRN2", target_bir_lowering=False, num_devices=1)
    t = [nc.dram_tensor(f"in_{n}", v.shape, mybir.dt.from_np(v.dtype), kind="ExternalInput").ap() for n, v in ins.items()]
    o = [nc.dram_tensor(f"out_{n}", s, mybir.dt.float32, kind="ExternalOutput").ap() for n, s in outs.items()]
    layer(nc, *t, *o)
    r = run_bass_kernel_spmd(nc, [{f"in_{k}": v for k, v in ins.items()}], core_ids=[0]).results[0]

    def tokens(v):
        return v.transpose(2, 1, 0).reshape(v.shape[2], -1)

    y, k, v, sh = (tokens(r[f"out_{n}"]) for n in ("y", "k", "v", "shift_rows"))
    w = r["out_wkv"].reshape(4, 2, 64, 2, 64)
    wkv = np.stack([w[:, h, :, h, :] for h in range(2)], 1).reshape(8, 64, 64).transpose(0, 2, 1)
    wkv_d = r["out_wkv_decode"].reshape(4, 2, 64, DEC, 64).transpose(3, 0, 1, 4, 2).reshape(1, DEC, 8, 64, 64)
    c = np.ascontiguousarray
    return (c(y[None, :SEQ]), c(y[SEQ:, None]), c(k[:SEQ].reshape(1, 1, SEQ, 4, P)), c(v[:SEQ].reshape(1, 1, SEQ, 4, P)),
            c(wkv[None, None]), c(sh[:1].reshape(1, 1, 1, RW_PROJ)), c(k[SEQ:].reshape(1, DEC, 1, 4, P)),
            c(v[SEQ:].reshape(1, DEC, 1, 4, P)), c(wkv_d), c(sh[1:].reshape(1, DEC, 1, RW_PROJ)))
```
